# Optimizing a Trainium2 kernel written in Bass

```python
import math
import jax, jax.numpy as jnp
from jax import lax
import numpy as np

D_MODEL = 1024
BATCH = 1
SEQ = 1024
DEPTH = 2

CTX_LEN = 256
GRID_W = 64
INNER = D_MODEL
HEAD_DIM = 64
A_WIDTH = INNER // 2
B_WIDTH = INNER - A_WIDTH
B_HEADS = B_WIDTH // HEAD_DIM
B_KV_HEADS = B_HEADS // 4
KV_WIDTH = B_KV_HEADS * HEAD_DIM
CONV_WIDTH = 31
Q_BLOCK = 128
ROPE_THETA = 10000.0
C_WIDTH = INNER // 2
C_GROUPS = 4
C_GROUP_DIM = C_WIDTH // C_GROUPS
D_WIDTH = INNER - C_WIDTH
D_HEADS = D_WIDTH // HEAD_DIM
NA_ROWS = 8
NA_COLS = 16
EPS = 1e-6
NEG_INF = -1e30
N_AB = (DEPTH + 1) // 2
N_CD = DEPTH // 2

AB_Q_OFF = 2 * A_WIDTH
AB_K_OFF = AB_Q_OFF + B_WIDTH
AB_V_OFF = AB_K_OFF + KV_WIDTH
AB_Z_OFF = AB_V_OFF + KV_WIDTH
AB_IN = AB_Z_OFF + INNER
CD_Q_OFF = C_WIDTH
CD_K_OFF = CD_Q_OFF + D_WIDTH
CD_V_OFF = CD_K_OFF + D_WIDTH
CD_Z_OFF = CD_V_OFF + D_WIDTH
CD_IN = CD_Z_OFF + INNER


def rms_norm(x, g):
    x32 = x.astype(jnp.float32)
    y = x32 * lax.rsqrt(jnp.mean(x32 * x32, axis=-1, keepdims=True) + EPS)
    return (y * g.astype(jnp.float32)).astype(x.dtype)

def layer_norm(x, g, b):
    x32 = x.astype(jnp.float32)
    mu = jnp.mean(x32, axis=-1, keepdims=True)
    xc = x32 - mu
    y = xc * lax.rsqrt(jnp.mean(xc * xc, axis=-1, keepdims=True) + EPS)
    return (y * g.astype(jnp.float32) + b.astype(jnp.float32)).astype(x.dtype)

def adaln(cond, w, b):
    m = jax.nn.silu(cond) @ w + b
    return jnp.split(m, 3, axis=-1)

def axial_rope(x):
    S = x.shape[1]
    t = jnp.arange(S)
    row = (t // GRID_W).astype(jnp.float32)
    col = (t % GRID_W).astype(jnp.float32)
    nf = HEAD_DIM // 4
    inv = ROPE_THETA ** (-jnp.arange(nf, dtype=jnp.float32) / nf)
    ang = jnp.concatenate([row[:, None] * inv, col[:, None] * inv], axis=-1)
    cos = jnp.cos(ang)[None, :, None, :]
    sin = jnp.sin(ang)[None, :, None, :]
    xp = x.astype(jnp.float32).reshape(x.shape[:-1] + (HEAD_DIM // 2, 2))
    a, b = xp[..., 0], xp[..., 1]
    out = jnp.stack([a * cos - b * sin, a * sin + b * cos], axis=-1)
    return out.reshape(x.shape).astype(x.dtype)

def dense_attn(q, k, v):
    Bq, Lq, Hq, dh = q.shape
    Hk = k.shape[2]
    qg = q.reshape(Bq, Lq, Hk, Hq // Hk, dh)
    s = jnp.einsum('bqkgd,bskd->bkgqs', qg, k).astype(jnp.float32) * (dh ** -0.5)
    p = jax.nn.softmax(s, axis=-1).astype(v.dtype)
    o = jnp.einsum('bkgqs,bskd->bqkgd', p, v)
    return o.reshape(Bq, Lq, Hq * dh)

def blocked_attn(q, k, v):
    Bq, S, Hq, dh = q.shape
    nb = S // Q_BLOCK
    qb = q.reshape(Bq, nb, Q_BLOCK, Hq, dh).transpose(1, 0, 2, 3, 4)
    ob = lax.map(lambda qi: dense_attn(qi, k, v), qb)
    return ob.transpose(1, 0, 2, 3).reshape(Bq, S, Hq * dh)

def dwconv(x, w, b):
    K = w.shape[0]
    y = lax.conv_general_dilated(x, w[:, None, :].astype(x.dtype), (1,), [(K // 2, K // 2)],
                                 dimension_numbers=('NWC', 'WIO', 'NWC'),
                                 feature_group_count=x.shape[-1])
    return y + b

def conformer_conv(a_val, a_gate, conv_w, conv_b, ln_g, ln_b):
    u = a_val * jax.nn.sigmoid(a_gate)
    u = dwconv(u, conv_w, conv_b)
    return jax.nn.silu(layer_norm(u, ln_g, ln_b))

def fourier_mix(f, w_c):
    Bf, L, _ = f.shape
    fg = f.reshape(Bf, L, C_GROUPS, C_GROUP_DIM).astype(jnp.float32)
    fr = jnp.fft.fft2(fg, axes=(1, 3), norm='ortho').real.astype(f.dtype)
    return jnp.einsum('blgc,gce->blge', fr, w_c).reshape(Bf, L, C_WIDTH)

def neighborhood_attn(q, k, v, kc, vc, rpb):
    Bq, S, H, dh = q.shape
    rows = S // GRID_W
    kr = min(NA_ROWS, rows)
    qg = q.reshape(Bq, rows, GRID_W, H, dh)
    kg = k.reshape(Bq, rows, GRID_W, H, dh)
    vg = v.reshape(Bq, rows, GRID_W, H, dh)
    r = jnp.arange(rows)
    rs = jnp.clip(r - kr // 2, 0, rows - kr)
    row_idx = rs[:, None] + jnp.arange(kr)[None, :]
    kb = kg[:, row_idx]
    vb = vg[:, row_idx]
    wq = jnp.arange(GRID_W)
    cs = jnp.clip(wq - NA_COLS // 2, 0, GRID_W - NA_COLS)
    col_ok = (wq[None, :] >= cs[:, None]) & (wq[None, :] < cs[:, None] + NA_COLS)
    dr_idx = row_idx - r[:, None] + (NA_ROWS - 1)
    dc_idx = jnp.clip(wq[None, :] - wq[:, None] + (NA_COLS - 1), 0, 2 * NA_COLS - 2)
    bias = rpb[:, dr_idx[:, None, :, None], dc_idx[None, :, None, :]]
    scale = dh ** -0.5
    s_win = jnp.einsum('brqhd,brkwhd->bhrqkw', qg, kb).astype(jnp.float32) * scale \
        + bias.astype(jnp.float32)[None]
    s_win = jnp.where(col_ok[:, None, :], s_win, NEG_INF).reshape(Bq, H, rows, GRID_W, kr * GRID_W)
    s_ctx = jnp.einsum('brqhd,bchd->bhrqc', qg, kc).astype(jnp.float32) * scale
    p = jax.nn.softmax(jnp.concatenate([s_win, s_ctx], axis=-1), axis=-1).astype(v.dtype)
    p_win = p[..., :kr * GRID_W].reshape(Bq, H, rows, GRID_W, kr, GRID_W)
    p_ctx = p[..., kr * GRID_W:]
    o = jnp.einsum('bhrqkw,brkwhd->brqhd', p_win, vb) + jnp.einsum('bhrqc,bchd->brqhd', p_ctx, vc)
    return o.reshape(Bq, S, H * dh)

def layer_ab(x, xc, c, c_ctx, w_ada, b_ada, norm_g, w_in, conv_w, conv_b, ln_g, ln_b,
             qn_g, kn_g, w_out, need_ctx):
    Bx, S, _ = x.shape
    L = xc.shape[1]
    shift, scale, gate = adaln(c[:, None, :], w_ada, b_ada)
    cshift, cscale, cgate = adaln(c_ctx, w_ada, b_ada)
    h = rms_norm(x, norm_g) * (1 + scale) + shift
    hc = rms_norm(xc, norm_g) * (1 + cscale) + cshift
    u = h @ w_in
    a_val, a_gate = u[..., :A_WIDTH], u[..., A_WIDTH:AB_Q_OFF]
    q = u[..., AB_Q_OFF:AB_K_OFF].reshape(Bx, S, B_HEADS, HEAD_DIM)
    k = u[..., AB_K_OFF:AB_V_OFF].reshape(Bx, S, B_KV_HEADS, HEAD_DIM)
    v = u[..., AB_V_OFF:AB_Z_OFF].reshape(Bx, S, B_KV_HEADS, HEAD_DIM)
    z = u[..., AB_Z_OFF:]
    uc = hc @ (w_in if need_ctx else w_in[:, AB_K_OFF:AB_Z_OFF])
    kv_off = AB_K_OFF if need_ctx else 0
    ck = uc[..., kv_off:kv_off + KV_WIDTH].reshape(Bx, L, B_KV_HEADS, HEAD_DIM)
    cv = uc[..., kv_off + KV_WIDTH:kv_off + 2 * KV_WIDTH].reshape(Bx, L, B_KV_HEADS, HEAD_DIM)
    ck = rms_norm(ck, kn_g)
    q = axial_rope(rms_norm(q, qn_g))
    k = axial_rope(rms_norm(k, kn_g))
    y_b = blocked_attn(q, jnp.concatenate([ck, k], axis=1), jnp.concatenate([cv, v], axis=1))
    y_a = conformer_conv(a_val, a_gate, conv_w, conv_b, ln_g, ln_b)
    y = jnp.concatenate([y_a, y_b], axis=-1) * jax.nn.silu(z)
    x = x + gate * (y @ w_out)
    if need_ctx:
        cq = rms_norm(uc[..., AB_Q_OFF:AB_K_OFF].reshape(Bx, L, B_HEADS, HEAD_DIM), qn_g)
        yc_b = dense_attn(cq, ck, cv)
        yc_a = conformer_conv(uc[..., :A_WIDTH], uc[..., A_WIDTH:AB_Q_OFF], conv_w, conv_b, ln_g, ln_b)
        yc = jnp.concatenate([yc_a, yc_b], axis=-1) * jax.nn.silu(uc[..., AB_Z_OFF:])
        xc = xc + cgate * (yc @ w_out)
    return x, xc

def layer_cd(x, xc, c, c_ctx, w_ada, b_ada, norm_g, w_in, w_fourier, rpb, w_out, need_ctx):
    Bx, S, _ = x.shape
    L = xc.shape[1]
    shift, scale, gate = adaln(c[:, None, :], w_ada, b_ada)
    cshift, cscale, cgate = adaln(c_ctx, w_ada, b_ada)
    h = rms_norm(x, norm_g) * (1 + scale) + shift
    hc = rms_norm(xc, norm_g) * (1 + cscale) + cshift
    u = h @ w_in
    f = u[..., :C_WIDTH]
    q = u[..., CD_Q_OFF:CD_K_OFF].reshape(Bx, S, D_HEADS, HEAD_DIM)
    k = u[..., CD_K_OFF:CD_V_OFF].reshape(Bx, S, D_HEADS, HEAD_DIM)
    v = u[..., CD_V_OFF:CD_Z_OFF].reshape(Bx, S, D_HEADS, HEAD_DIM)
    z = u[..., CD_Z_OFF:]
    uc = hc @ (w_in if need_ctx else w_in[:, CD_K_OFF:CD_Z_OFF])
    kv_off = CD_K_OFF if need_ctx else 0
    ck = uc[..., kv_off:kv_off + D_WIDTH].reshape(Bx, L, D_HEADS, HEAD_DIM)
    cv = uc[..., kv_off + D_WIDTH:kv_off + 2 * D_WIDTH].reshape(Bx, L, D_HEADS, HEAD_DIM)
    y_c = fourier_mix(f, w_fourier)
    y_d = neighborhood_attn(q, k, v, ck, cv, rpb)
    y = jnp.concatenate([y_c, y_d], axis=-1) * jax.nn.silu(z)
    x = x + gate * (y @ w_out)
    if need_ctx:
        cq = uc[..., CD_Q_OFF:CD_K_OFF].reshape(Bx, L, D_HEADS, HEAD_DIM)
        yc_d = dense_attn(cq, ck, cv)
        yc_c = fourier_mix(uc[..., :C_WIDTH], w_fourier)
        yc = jnp.concatenate([yc_c, yc_d], axis=-1) * jax.nn.silu(uc[..., CD_Z_OFF:])
        xc = xc + cgate * (yc @ w_out)
    return x, xc

def first_inputs(seed: int = 0) -> dict:
    key = jax.random.key(seed)
    ks = iter(jax.random.split(key, 32))
    nrm = lambda shape, s: jax.random.normal(next(ks), shape, jnp.float32) * s
    gain = lambda shape: 1.0 + nrm(shape, 0.05)
    return {
        "x": nrm((BATCH, SEQ, D_MODEL), 1.0),
        "c": nrm((BATCH, D_MODEL), 1.0),
        "ctx": nrm((BATCH, CTX_LEN, D_MODEL), 1.0),
        "c_ctx": nrm((D_MODEL,), 1.0),
        "ab_w_ada": nrm((N_AB, D_MODEL, 3 * D_MODEL), 0.5 * D_MODEL ** -0.5),
        "ab_b_ada": nrm((N_AB, 3 * D_MODEL), 0.01),
        "ab_norm_g": gain((N_AB, D_MODEL)),
        "ab_w_in": nrm((N_AB, D_MODEL, AB_IN), D_MODEL ** -0.5),
        "ab_conv_w": nrm((N_AB, CONV_WIDTH, A_WIDTH), CONV_WIDTH ** -0.5),
        "ab_conv_b": nrm((N_AB, A_WIDTH), 0.01),
        "ab_ln_g": gain((N_AB, A_WIDTH)),
        "ab_ln_b": nrm((N_AB, A_WIDTH), 0.01),
        "ab_q_norm_g": gain((N_AB, HEAD_DIM)),
        "ab_k_norm_g": gain((N_AB, HEAD_DIM)),
        "ab_w_out": nrm((N_AB, INNER, D_MODEL), INNER ** -0.5),
        "cd_w_ada": nrm((N_CD, D_MODEL, 3 * D_MODEL), 0.5 * D_MODEL ** -0.5),
        "cd_b_ada": nrm((N_CD, 3 * D_MODEL), 0.01),
        "cd_norm_g": gain((N_CD, D_MODEL)),
        "cd_w_in": nrm((N_CD, D_MODEL, CD_IN), D_MODEL ** -0.5),
        "cd_w_fourier": nrm((N_CD, C_GROUPS, C_GROUP_DIM, C_GROUP_DIM), C_GROUP_DIM ** -0.5),
        "cd_rpb": nrm((N_CD, D_HEADS, 2 * NA_ROWS - 1, 2 * NA_COLS - 1), 0.1),
        "cd_w_out": nrm((N_CD, INNER, D_MODEL), INNER ** -0.5),
        "final_norm_g": gain((D_MODEL,)),
    }

def first_block(x, c, ctx, c_ctx, ab_w_ada, ab_b_ada, ab_norm_g, ab_w_in, ab_conv_w, ab_conv_b,
              ab_ln_g, ab_ln_b, ab_q_norm_g, ab_k_norm_g, ab_w_out, cd_w_ada, cd_b_ada, cd_norm_g,
              cd_w_in, cd_w_fourier, cd_rpb, cd_w_out, final_norm_g):
    xc = ctx
    for layer in range(DEPTH):
        need_ctx = layer < DEPTH - 1
        i = layer // 2
        if layer % 2 == 0:
            x, xc = layer_ab(x, xc, c, c_ctx, ab_w_ada[i], ab_b_ada[i], ab_norm_g[i], ab_w_in[i],
                             ab_conv_w[i], ab_conv_b[i], ab_ln_g[i], ab_ln_b[i],
                             ab_q_norm_g[i], ab_k_norm_g[i], ab_w_out[i], need_ctx)
        else:
            x, xc = layer_cd(x, xc, c, c_ctx, cd_w_ada[i], cd_b_ada[i], cd_norm_g[i], cd_w_in[i],
                             cd_w_fourier[i], cd_rpb[i], cd_w_out[i], need_ctx)
    return rms_norm(x, final_norm_g)


N_Q_HEADS = 8
N_KV_HEADS = 2
GQA_GROUP = N_Q_HEADS // N_KV_HEADS
WINDOW = 128
ATT_BLOCK = 128
ROPE_BASE = 10000.0
Q_DIM = N_Q_HEADS * HEAD_DIM
KV_DIM = N_KV_HEADS * HEAD_DIM
SG_GROUPS = 8
SG_HEAD = 64
SG_WIDTH = SG_GROUPS * SG_HEAD
SG_CHUNK = 128
EVEN_IN = Q_DIM + 2 * KV_DIM + 2 * SG_WIDTH
EVEN_MIX = Q_DIM + SG_WIDTH
CONV_WIDTH_2 = D_MODEL
CONV_K = 3
N_GROUPS = 4
EXPERTS_PER_GROUP = 8
N_EXPERTS = N_GROUPS * EXPERTS_PER_GROUP
TOP_K_IN_GROUP = 2
EXPERT_HIDDEN = D_MODEL // 2
MOE_BLOCK = 128
N_EVEN = (DEPTH + 1) // 2
N_ODD = DEPTH // 2
NEG_INF_2 = -1e30


def rms_norm_2(x, g):
    xf = x.astype(jnp.float32)
    y = xf * lax.rsqrt(jnp.mean(xf * xf, axis=-1, keepdims=True) + EPS)
    return (y * g.astype(jnp.float32)).astype(x.dtype)

def layer_norm_2(x, g):
    xf = x.astype(jnp.float32)
    mu = jnp.mean(xf, axis=-1, keepdims=True)
    xc = xf - mu
    y = xc * lax.rsqrt(jnp.mean(xc * xc, axis=-1, keepdims=True) + EPS)
    return (y * g.astype(jnp.float32)).astype(x.dtype)

def modulate(h, shift, scale):
    return h * (1 + scale) + shift

def axial_rope_tables(rows, dtype):
    quarter = HEAD_DIM // 4
    row_ids = jnp.repeat(jnp.arange(rows, dtype=jnp.float32), GRID_W)
    col_ids = jnp.tile(jnp.arange(GRID_W, dtype=jnp.float32), rows)
    inv = ROPE_BASE ** (-jnp.arange(quarter, dtype=jnp.float32) / quarter)
    ang_r = row_ids[:, None] * inv
    ang_c = col_ids[:, None] * inv
    return (jnp.cos(ang_r)[:, None, :].astype(dtype), jnp.sin(ang_r)[:, None, :].astype(dtype),
            jnp.cos(ang_c)[:, None, :].astype(dtype), jnp.sin(ang_c)[:, None, :].astype(dtype))

def apply_axial_rope(t, rope):
    cos_r, sin_r, cos_c, sin_c = rope
    half = HEAD_DIM // 2
    quarter = HEAD_DIM // 4

    def rot(u, cos, sin):
        u1, u2 = u[..., :quarter], u[..., quarter:]
        return jnp.concatenate([u1 * cos - u2 * sin, u2 * cos + u1 * sin], axis=-1)

    return jnp.concatenate([rot(t[..., :half], cos_r, sin_r), rot(t[..., half:], cos_c, sin_c)], axis=-1)

def windowed_attention(q, k, v, kc, vc, sink):
    b, s = q.shape[:2]
    nb = s // ATT_BLOCK
    scale = HEAD_DIM ** -0.5
    f32 = jnp.float32
    qb = q.reshape(b, nb, ATT_BLOCK, N_KV_HEADS, GQA_GROUP, HEAD_DIM)

    def band(t):
        tp = jnp.pad(t, ((0, 0), (ATT_BLOCK, ATT_BLOCK), (0, 0), (0, 0)))
        tp = tp.reshape(b, nb + 2, ATT_BLOCK, N_KV_HEADS, HEAD_DIM)
        return jnp.concatenate([tp[:, :-2], tp[:, 1:-1], tp[:, 2:]], axis=2)

    kb, vb = band(k), band(v)
    s_loc = jnp.einsum('bnqhgd,bnkhd->bnhgqk', qb, kb, preferred_element_type=f32) * scale
    s_ctx = jnp.einsum('bnqhgd,bchd->bnhgqc', qb, kc, preferred_element_type=f32) * scale
    qi = jnp.arange(ATT_BLOCK)[:, None]
    kj = jnp.arange(3 * ATT_BLOCK)[None, :]
    in_win = jnp.abs(kj - qi - ATT_BLOCK) <= WINDOW
    kpos = (jnp.arange(nb)[:, None] - 1) * ATT_BLOCK + jnp.arange(3 * ATT_BLOCK)[None, :]
    mask = in_win[None] & ((kpos >= 0) & (kpos < s))[:, None, :]
    s_loc = jnp.where(mask[None, :, None, None], s_loc, NEG_INF_2)
    sink_l = jnp.broadcast_to(sink.astype(f32).reshape(1, 1, N_KV_HEADS, GQA_GROUP, 1, 1), s_ctx.shape[:-1] + (1,))
    p = jax.nn.softmax(jnp.concatenate([sink_l, s_ctx, s_loc], axis=-1), axis=-1)
    n_ctx = kc.shape[1]
    p_ctx = p[..., 1:1 + n_ctx].astype(vc.dtype)
    p_loc = p[..., 1 + n_ctx:].astype(vb.dtype)
    o = (jnp.einsum('bnhgqc,bchd->bnqhgd', p_ctx, vc)
         + jnp.einsum('bnhgqk,bnkhd->bnqhgd', p_loc, vb))
    return o.reshape(b, s, Q_DIM)

def context_attention(qc, kc, vc, sink):
    b, n = qc.shape[:2]
    f32 = jnp.float32
    qh = qc.reshape(b, n, N_KV_HEADS, GQA_GROUP, HEAD_DIM)
    sc = jnp.einsum('bqhgd,bkhd->bhgqk', qh, kc, preferred_element_type=f32) * (HEAD_DIM ** -0.5)
    sink_c = jnp.broadcast_to(sink.astype(f32).reshape(1, N_KV_HEADS, GQA_GROUP, 1, 1), sc.shape[:-1] + (1,))
    p = jax.nn.softmax(jnp.concatenate([sink_c, sc], axis=-1), axis=-1)
    o = jnp.einsum('bhgqk,bkhd->bqhgd', p[..., 1:].astype(vc.dtype), vc)
    return o.reshape(b, n, Q_DIM)

def spatial_gating(u, z, g_sgu, w_sp, b_sp):
    b, n = u.shape[:2]
    u = jax.nn.gelu(u, approximate=False)
    z = layer_norm_2(jax.nn.gelu(z, approximate=False), g_sgu)
    zc = z.reshape(b, n // SG_CHUNK, SG_CHUNK, SG_GROUPS, SG_HEAD)
    sgate = jnp.einsum('hij,bnjhc->bnihc', w_sp, zc) + b_sp.T[:, :, None]
    return (u.reshape(zc.shape) * sgate).reshape(b, n, SG_WIDTH)

def even_mixer(h, hc, w_in, sink, g_sgu, w_sp, b_sp, w_out, rope, need_ctx):
    b, s, _ = h.shape
    n_ctx = hc.shape[1]
    q, k, v, u, z = jnp.split(h @ w_in, [Q_DIM, Q_DIM + KV_DIM, Q_DIM + 2 * KV_DIM, Q_DIM + 2 * KV_DIM + SG_WIDTH], axis=-1)
    q = apply_axial_rope(q.reshape(b, s, N_Q_HEADS, HEAD_DIM), rope)
    k = apply_axial_rope(k.reshape(b, s, N_KV_HEADS, HEAD_DIM), rope)
    v = v.reshape(b, s, N_KV_HEADS, HEAD_DIM)
    kc, vc = jnp.split(hc @ w_in[:, Q_DIM:Q_DIM + 2 * KV_DIM], 2, axis=-1)
    kc = kc.reshape(b, n_ctx, N_KV_HEADS, HEAD_DIM)
    vc = vc.reshape(b, n_ctx, N_KV_HEADS, HEAD_DIM)
    att = windowed_attention(q, k, v, kc, vc, sink)
    sg = spatial_gating(u, z, g_sgu, w_sp, b_sp)
    out_lat = jnp.concatenate([att, sg], axis=-1) @ w_out
    if not need_ctx:
        return out_lat, None
    qc = hc @ w_in[:, :Q_DIM]
    uc, zc = jnp.split(hc @ w_in[:, Q_DIM + 2 * KV_DIM:], 2, axis=-1)
    att_c = context_attention(qc, kc, vc, sink)
    sg_c = spatial_gating(uc, zc, g_sgu, w_sp, b_sp)
    return out_lat, jnp.concatenate([att_c, sg_c], axis=-1) @ w_out

def short_conv_mixer(h, w_in, conv_w, w_out):
    bg, cg, xt = jnp.split(h @ w_in, 3, axis=-1)
    y = cg * xt
    yp = jnp.pad(y, ((0, 0), (1, 1), (0, 0)))
    conv = yp[:, :-2] * conv_w[0] + yp[:, 1:-1] * conv_w[1] + yp[:, 2:] * conv_w[2]
    return (bg * conv) @ w_out

def moe_ffn(h, w_rg, b_rg, w_re, b_re, w_gate, w_up, w_down):
    n, d = h.shape
    f32 = jnp.float32
    g_logits = jnp.einsum('nd,dg->ng', h, w_rg, preferred_element_type=f32) + b_rg.astype(f32)
    g_idx = jnp.argmax(g_logits, axis=-1).astype(jnp.int32)
    g_w = jnp.take_along_axis(jax.nn.softmax(g_logits, axis=-1), g_idx[:, None], axis=-1)
    e_logits = (jnp.einsum('nd,de->ne', h, w_re, preferred_element_type=f32) + b_re.astype(f32))
    e_logits = e_logits.reshape(n, N_GROUPS, EXPERTS_PER_GROUP)
    e_sel = jnp.take_along_axis(e_logits, g_idx[:, None, None], axis=1)[:, 0]
    top_v, top_i = lax.top_k(e_sel, TOP_K_IN_GROUP)
    gate = g_w * jax.nn.softmax(top_v, axis=-1)
    expert = g_idx[:, None] * EXPERTS_PER_GROUP + top_i.astype(jnp.int32)
    n_assign = n * TOP_K_IN_GROUP
    flat_e = expert.reshape(-1)
    flat_tok = jnp.repeat(jnp.arange(n, dtype=jnp.int32), TOP_K_IN_GROUP)
    flat_w = gate.reshape(-1).astype(h.dtype)
    order = jnp.argsort(flat_e)
    sorted_e = flat_e[order]
    counts = jnp.bincount(flat_e, length=N_EXPERTS)
    padded = (counts + MOE_BLOCK - 1) // MOE_BLOCK * MOE_BLOCK
    pad_end = jnp.cumsum(padded)
    pad_start = pad_end - padded
    raw_start = jnp.cumsum(counts) - counts
    dest = pad_start[sorted_e] + jnp.arange(n_assign, dtype=pad_start.dtype) - raw_start[sorted_e]
    n_blocks = -(-n_assign // MOE_BLOCK) + N_EXPERTS
    n_rows = n_blocks * MOE_BLOCK
    row_tok = jnp.zeros((n_rows,), jnp.int32).at[dest].set(flat_tok[order])
    row_w = jnp.zeros((n_rows,), h.dtype).at[dest].set(flat_w[order])
    block_e = jnp.clip(jnp.searchsorted(pad_end, jnp.arange(n_blocks, dtype=pad_end.dtype) * MOE_BLOCK, side='right'), 0, N_EXPERTS - 1)
    xb = h[row_tok].reshape(n_blocks, MOE_BLOCK, d)

    def expert_block(args):
        xblk, e = args
        hid = jax.nn.silu(xblk @ w_gate[e]) * (xblk @ w_up[e])
        return hid @ w_down[e]

    yb = lax.map(expert_block, (xb, block_e)).reshape(n_rows, d)
    return jnp.zeros_like(h).at[row_tok].add(yb * row_w[:, None])

def second_inputs(seed: int = 0) -> dict:
    key = jax.random.key(seed)
    ks = jax.random.split(key, 25)
    D = D_MODEL

    def nrm(k, shape, s):
        return jax.random.normal(k, shape, jnp.float32) * s

    return {
        'x': nrm(ks[0], (BATCH, SEQ, D), 1.0),
        'c': nrm(ks[1], (BATCH, D), 1.0),
        'ctx': nrm(ks[2], (BATCH, CTX_LEN, D), 1.0),
        'c_ctx': nrm(ks[3], (D,), 1.0),
        'w_ada': nrm(ks[4], (DEPTH, D, 6 * D), 0.5 * D ** -0.5),
        'b_ada': nrm(ks[5], (DEPTH, 6 * D), 0.02),
        'g_norm1': 1.0 + nrm(ks[6], (DEPTH, D), 0.1),
        'g_norm2': 1.0 + nrm(ks[7], (DEPTH, D), 0.1),
        'g_final': 1.0 + nrm(ks[8], (D,), 0.1),
        'w_in_even': nrm(ks[9], (N_EVEN, D, EVEN_IN), D ** -0.5),
        'attn_sink': nrm(ks[10], (N_EVEN, N_Q_HEADS), 1.0),
        'g_sgu': 1.0 + nrm(ks[11], (N_EVEN, SG_WIDTH), 0.1),
        'w_spatial': nrm(ks[12], (N_EVEN, SG_GROUPS, SG_CHUNK, SG_CHUNK), SG_CHUNK ** -0.5),
        'b_spatial': 1.0 + nrm(ks[13], (N_EVEN, SG_GROUPS, SG_CHUNK), 0.1),
        'w_out_even': nrm(ks[14], (N_EVEN, EVEN_MIX, D), EVEN_MIX ** -0.5),
        'w_in_odd': nrm(ks[15], (N_ODD, D, 3 * CONV_WIDTH_2), D ** -0.5),
        'conv_w': nrm(ks[16], (N_ODD, CONV_K, CONV_WIDTH_2), CONV_K ** -0.5),
        'w_out_odd': nrm(ks[17], (N_ODD, CONV_WIDTH_2, D), CONV_WIDTH_2 ** -0.5),
        'w_router_group': nrm(ks[18], (DEPTH, D, N_GROUPS), D ** -0.5),
        'b_router_group': nrm(ks[19], (DEPTH, N_GROUPS), 0.01),
        'w_router_expert': nrm(ks[20], (DEPTH, D, N_EXPERTS), D ** -0.5),
        'b_router_expert': nrm(ks[21], (DEPTH, N_EXPERTS), 0.01),
        'w_gate': nrm(ks[22], (DEPTH, N_EXPERTS, D, EXPERT_HIDDEN), D ** -0.5),
        'w_up': nrm(ks[23], (DEPTH, N_EXPERTS, D, EXPERT_HIDDEN), D ** -0.5),
        'w_down': nrm(ks[24], (DEPTH, N_EXPERTS, EXPERT_HIDDEN, D), EXPERT_HIDDEN ** -0.5),
    }

def second_block(x, c, ctx, c_ctx, w_ada, b_ada, g_norm1, g_norm2, g_final, w_in_even, attn_sink, g_sgu,
              w_spatial, b_spatial, w_out_even, w_in_odd, conv_w, w_out_odd, w_router_group,
              b_router_group, w_router_expert, b_router_expert, w_gate, w_up, w_down):
    b, s, d = x.shape
    rows = s // GRID_W
    rope = axial_rope_tables(rows, x.dtype)
    silu_c = jax.nn.silu(c)
    silu_cc = jax.nn.silu(c_ctx)
    lat, cx = x, ctx
    for l in range(DEPTH):
        need_ctx = any(j % 2 == 0 for j in range(l + 1, DEPTH))
        m = jnp.split(silu_c @ w_ada[l] + b_ada[l], 6, axis=-1)
        sh1, sc1, g1, sh2, sc2, g2 = [t[:, None, :] for t in m]
        h = modulate(rms_norm_2(lat, g_norm1[l]), sh1, sc1)
        mix_c = None
        if l % 2 == 0 or need_ctx:
            csh1, csc1, cg1, csh2, csc2, cg2 = jnp.split(silu_cc @ w_ada[l] + b_ada[l], 6, axis=-1)
            hc = modulate(rms_norm_2(cx, g_norm1[l]), csh1, csc1)
        i = l // 2
        if l % 2 == 0:
            mix, mix_c = even_mixer(h, hc, w_in_even[i], attn_sink[i], g_sgu[i], w_spatial[i],
                                    b_spatial[i], w_out_even[i], rope, need_ctx)
        else:
            mix = short_conv_mixer(h, w_in_odd[i], conv_w[i], w_out_odd[i])
            if need_ctx:
                mix_c = short_conv_mixer(hc, w_in_odd[i], conv_w[i], w_out_odd[i])
        lat = lat + g1 * mix
        h2 = modulate(rms_norm_2(lat, g_norm2[l]), sh2, sc2)
        lat = lat + g2 * moe_ffn(h2.reshape(-1, d), w_router_group[l], b_router_group[l], w_router_expert[l],
                                 b_router_expert[l], w_gate[l], w_up[l], w_down[l]).reshape(b, s, d)
        if need_ctx:
            cx = cx + cg1 * mix_c
            hc2 = modulate(rms_norm_2(cx, g_norm2[l]), csh2, csc2)
            cx = cx + cg2 * moe_ffn(hc2.reshape(-1, d), w_router_group[l], b_router_group[l], w_router_expert[l],
                                    b_router_expert[l], w_gate[l], w_up[l], w_down[l]).reshape(cx.shape)
    return rms_norm_2(lat, g_final)


def setup_inputs(seed=0):
    out = dict(first_inputs(seed))
    for name, value in second_inputs(seed + 1).items():
        if name != "x":
            out[name + "_2"] = value
    return out


def reference(
    x, c, ctx, c_ctx, ab_w_ada, ab_b_ada, ab_norm_g, ab_w_in, ab_conv_w, ab_conv_b, ab_ln_g,
    ab_ln_b, ab_q_norm_g, ab_k_norm_g, ab_w_out, cd_w_ada, cd_b_ada, cd_norm_g, cd_w_in,
    cd_w_fourier, cd_rpb, cd_w_out, final_norm_g, c_2, ctx_2, c_ctx_2, w_ada_2, b_ada_2,
    g_norm1_2, g_norm2_2, g_final_2, w_in_even_2, attn_sink_2, g_sgu_2, w_spatial_2,
    b_spatial_2, w_out_even_2, w_in_odd_2, conv_w_2, w_out_odd_2, w_router_group_2,
    b_router_group_2, w_router_expert_2, b_router_expert_2, w_gate_2, w_up_2, w_down_2,
):
    x = first_block(
        x, c, ctx, c_ctx, ab_w_ada, ab_b_ada, ab_norm_g, ab_w_in, ab_conv_w, ab_conv_b, ab_ln_g,
        ab_ln_b, ab_q_norm_g, ab_k_norm_g, ab_w_out, cd_w_ada, cd_b_ada, cd_norm_g, cd_w_in,
        cd_w_fourier, cd_rpb, cd_w_out, final_norm_g,
    )
    return second_block(
        x, c_2, ctx_2, c_ctx_2, w_ada_2, b_ada_2, g_norm1_2, g_norm2_2, g_final_2, w_in_even_2,
        attn_sink_2, g_sgu_2, w_spatial_2, b_spatial_2, w_out_even_2, w_in_odd_2, conv_w_2,
        w_out_odd_2, w_router_group_2, b_router_group_2, w_router_expert_2, b_router_expert_2,
        w_gate_2, w_up_2, w_down_2,
    )


_drawn_inputs = setup_inputs


def setup_inputs(seed=0):
    import zlib

    import numpy as np

    out = dict(_drawn_inputs(seed))
    spreads = {}
    factors = {'ctx': 2.861,
     'ab_b_ada': 6.345,
     'ab_norm_g': 4.344,
     'ab_conv_b': 8.0,
     'ab_ln_g': 5.725,
     'ab_ln_b': 8.0,
     'ab_q_norm_g': 8.0,
     'ab_k_norm_g': 8.0,
     'cd_b_ada': 6.418,
     'cd_norm_g': 4.1,
     'cd_rpb': 8.0,
     'ctx_2': 8.21,
     'attn_sink_2': 8.0,
     'b_router_group_2': 18.726,
     'b_router_expert_2': 17.352}
    for name, (base, spread) in spreads.items():
        noise = np.random.default_rng([zlib.crc32(name.encode()), seed]).standard_normal(out[name].shape)
        drawn = base * np.exp(spread * noise) if base else spread * noise
        out[name] = __import__('jax').numpy.asarray(drawn.astype(out[name].dtype))
    for name, factor in factors.items():
        out[name] = (out[name] * factor).astype(out[name].dtype)
    return out
```

```python
from contextlib import ExitStack

import numpy as np
import concourse.bass as bass
from concourse import mybir

F32 = mybir.dt.float32
I32 = mybir.dt.int32
ALU = mybir.AluOpType
ACT = mybir.ActivationFunctionType
X_AXIS = mybir.AxisListType.X

P = 128
D = 1024
KT = D // P
S = 1024
L = 256
HEAD = 64
GRID = 64
ROWS = S // GRID
TAPS = 31
NA_ROWS, NA_COLS = 8, 16
RPB_R, RPB_C = 2 * NA_ROWS - 1, 2 * NA_COLS - 1
EPS = 1e-6
NEG = -1e30
SCALE = HEAD ** -0.5
E = 32
GROUPS, PER = 4, 8
HID = D // 2
BLK = 128
NBLK = 2 * S // BLK + E
NBLK += NBLK % 2
UNIT = KT * 512

VEC = {}
_at = 0
for _name, _n in (("ab_b_ada", 24), ("ab_norm_g", 8), ("ab_conv_w", 4 * TAPS), ("ab_conv_b", 4), ("ab_ln_g", 4),
                  ("ab_ln_b", 4), ("ab_qn_g", 1), ("ab_kn_g", 1), ("cd_b_ada", 24), ("cd_norm_g", 8),
                  ("final_g", 8), ("b_ada0", 48), ("b_ada1", 48), ("g_norm1_0", 8), ("g_norm1_1", 8),
                  ("g_norm2_0", 8), ("g_norm2_1", 8), ("g_final2", 8), ("conv3_w", 24), ("silu_in", 32)):
    VEC[_name] = (_at, _n)
    _at += _n
NVEC = _at

CONST = {}
_at = 0
for _name, _n in (("ident", 128), ("ones", 128), ("before", 128), ("swap_ab", 128), ("swap_ev", 128),
                  ("head_ones", 128), ("expert_before", 32), ("expert_upto", 32), ("full_blocks", S // BLK + 1),
                  ("iota4", 4), ("iota8", 8), ("iota_blk", NBLK), ("iota_pair", NBLK // 2), ("eps", 1)):
    CONST[_name] = (_at, _n)
    _at += _n
NCONST = _at


def program(nc, t):
    with ExitStack() as ctx:
        def sem(name):
            return ctx.enter_context(nc.semaphore(name))

        words = 53200
        arena = ctx.enter_context(nc.sbuf_tensor("arena", [P, words], F32))
        banks = ctx.enter_context(nc.psum_tensor("banks", [P, 8 * 512], F32))

        def mem(at, *dims, n=P):
            size = int(np.prod(dims))
            a = arena[0:n, at:at + size]
            if len(dims) == 2:
                return a.rearrange("p (a b) -> p a b", a=dims[0])
            if len(dims) == 3:
                return a.rearrange("p (a b c) -> p a b c", a=dims[0], b=dims[1])
            return a

        def bank(i, n=1):
            return banks[:, i * 512:(i + n) * 512]

        XT, HT, HC, YT, YC, XC, RING, KEEP = 0, 8192, 16384, 18432, 26624, 28672, 30720, 38912
        STAGE = words - 3 * UNIT
        x_l, h_l, y_l = (mem(a, KT, S) for a in (XT, HT, YT))
        x_c, h_c, y_c = (mem(a, KT, L) for a in (XC, HC, YC))
        ring = mem(RING, 2, UNIT)
        at = KEEP
        vec = mem(at, NVEC); at += NVEC
        cst = mem(at, NCONST); at += NCONST
        NMOD = {"ab": (24, 2), "cd": (24, 2), "l0": (48, 2), "l1": (48, 2)}
        mod = {}
        for name, (n, m) in NMOD.items():
            mod[name] = mem(at, n, m); at += n * m
        gs = {}
        for name in ("ab", "cd", "l0", "l0b", "l1", "l1b"):
            gs[name] = mem(at, KT, 2); at += 2 * KT
        SILU = at; at += 32
        moe_w = mem(at, 2, KT); at += 2 * KT
        moe_i = mem(at, 2, KT).bitcast(I32); at += 2 * KT
        moe_tab = mem(at, NBLK + 2).bitcast(I32); at += NBLK + 2
        moe_ix = mem(at, 2).bitcast(I32); at += 2
        row_ix = mem(at, NBLK).bitcast(I32); at += NBLK
        stat = mem(at, 4, 8); at += 32
        assert at <= STAGE, (at, STAGE)

        def v(name, i=0, n=1):
            a, m = VEC[name]
            assert i + n <= m
            return vec[:, a + i:a + i + n]

        def c(name, n=P):
            a, m = CONST[name]
            return cst[0:n, a:a + m]

        ident, ones, eps = c("ident"), c("ones"), c("eps")

        stage_end = sem("stage_end")
        loaded = sem("loaded")
        block = ctx.enter_context(nc.Block())

        def closer(eng):
            at_ = [0]

            def close(name):
                assert STAGES[at_[0]] == name
                at_[0] += 1
                eng.drain().then_inc(stage_end, 1)
                eng.wait_ge(stage_end, closed(name))
            return close

        ring_in = [sem(f"ring_in{i}") for i in range(2)]
        unit_used = {}

        units = []

        def add_units(name, mat, numbers, kv=None):
            for j in numbers:
                col = 512 * j - (256 if kv is not None and j > kv else 0)
                units.append((name, j, mat, col, 256 if j == kv else 512))

        add_units("ab_ada", t["ab_w_ada"], range(6))
        add_units("ab_in", t["ab_w_in"], (0, 1, 2, 3), 3)
        add_units("cd_ada", t["cd_w_ada"], range(6))
        add_units("l0_ada", t["w_ada0"], range(12))
        add_units("l1_ada", t["w_ada1"], range(12))
        add_units("ab_in", t["ab_w_in"], (4, 5), 3)
        add_units("ab_out", t["ab_w_out"], range(2))
        add_units("cd_in", t["cd_w_in"], (0,))
        for half in range(2):
            units.append(("four", 2 * half, t["four_cos"], 512 * half, 512))
            units.append(("four", 2 * half + 1, t["four_sin"], 512 * half, 512))
        add_units("cd_in", t["cd_w_in"], range(1, 6))
        add_units("cd_out", t["cd_w_out"], range(2))
        add_units("ev_in", t["w_in_even"], range(4), 1)
        add_units("ev_out", t["w_out_even"], range(2))
        UNITS_TO_MOE0 = len(units)
        add_units("od_in", t["w_in_odd"], range(6))
        add_units("od_out", t["w_out_odd"], range(2))
        unit_no = {(n, j): i for i, (n, j, *_) in enumerate(units)}

        def unit_wait(pe, name, j):
            n = unit_no[(name, j)]
            pe.wait_ge(ring_in[n % 2], 16 * (n // 2 + 1))
            return ring[:, n % 2].rearrange("p (k n) -> p k n", k=KT)

        class Group:
            def __init__(self, unit, cols, rows, kind, dst, **more):
                self.unit, self.cols, self.rows, self.kind, self.dst = unit, cols, rows, kind, dst
                self.more = more

        proj_mm = sem("proj_mm")
        proj_ev = {"A": sem("proj_ev_act"), "D": sem("proj_ev_dve")}
        half_out = sem("half_out")
        total = {"mm": 0, "A": 0, "D": 0, "half": 0}

        READER = {"copyA": "A", "copyD": "D", "gelu": "A", "sigmoid": "A", "times": "D", "silu": "A",
                  "resid": "D", "keep": "A", "conv": "D"}

        class Projection:
            def __init__(self, groups, per_unit, half=None):
                self.groups, self.half = groups, half
                self.mm0 = total["mm"]
                self.half_used, n_times = [], 0
                self.reader, self.nth = [], []
                count = {"A": total["A"], "D": total["D"]}
                for g in groups:
                    e = READER[g.kind]
                    count[e] += 1
                    self.reader.append(e)
                    self.nth.append(count[e])
                    unit_used[unit_no[g.unit]] = (proj_mm, self.mm0 + len(self.reader))
                    if g.kind in ("sigmoid", "silu", "keep"):
                        self.half_used.append(None)
                    if g.kind == "times":
                        self.half_used[n_times] = (proj_ev["D"], count["D"])
                        n_times += 1
                    if g.kind == "silu":
                        total["half"] += 1
                        self.half_used[-1] = (half_out, total["half"])
                total["mm"] += len(groups)
                total["A"], total["D"] = count["A"], count["D"]

            def pe(self, pe):
                for g, grp in enumerate(self.groups):
                    if g == 0 or self.groups[g - 1].unit != grp.unit:
                        wts = unit_wait(pe, *grp.unit)
                    if g >= 8:
                        pe.wait_ge(proj_ev[self.reader[g - 8]], self.nth[g - 8])
                    for k in range(KT):
                        if grp.rows[0] == "tok":
                            _, src, t0, n = grp.rows
                            lhsT, rhs = src[:, k, t0:t0 + P], wts[:, k, grp.cols[0]:grp.cols[1]]
                        else:
                            _, src, t0, n = grp.rows
                            lhsT, rhs = wts[:, k, grp.cols[0]:grp.cols[1]], src[:, k, t0:t0 + n]
                        last = pe.matmul(bank(g % 8)[:, 0:n], lhsT, rhs, start=k == 0, stop=k == KT - 1)
                    last.then_inc(proj_mm, 1)

            def act(self, a):
                halves = 0
                for g, grp in enumerate(self.groups):
                    if self.reader[g] != "A":
                        continue
                    n = grp.rows[3]
                    src = bank(g % 8)[:, 0:n]
                    a.wait_ge(proj_mm, self.mm0 + g + 1)
                    if grp.kind == "copyA":
                        a.activation(grp.dst, src, ACT.Copy).then_inc(proj_ev["A"], 1)
                    elif grp.kind == "gelu":
                        a.activation(grp.dst, src, ACT.Gelu).then_inc(proj_ev["A"], 1)
                    else:
                        if halves >= 4:
                            a.wait_ge(*self.half_used[halves - 4])
                        f = {"sigmoid": ACT.Sigmoid, "silu": ACT.Silu, "keep": ACT.Copy}[grp.kind]
                        a.activation(self.half[:, halves % 4, 0:n], src, f).then_inc(proj_ev["A"], 1)
                        halves += 1

            def dve(self, d):
                halves = 0
                for g, grp in enumerate(self.groups):
                    n = grp.rows[3]
                    src = bank(g % 8)[:, 0:n]
                    if grp.kind == "silu":
                        d.wait_ge(proj_ev["A"], self.nth[g])
                        d.tensor_tensor(grp.dst, grp.dst, self.half[:, halves % 4, 0:n],
                                        ALU.mult).then_inc(half_out, 1)
                        halves += 1
                    if self.reader[g] != "D":
                        continue
                    d.wait_ge(proj_mm, self.mm0 + g + 1)
                    if grp.kind == "copyD":
                        d.tensor_copy(grp.dst, src).then_inc(proj_ev["D"], 1)
                    elif grp.kind == "resid":
                        d.scalar_tensor_tensor(out=grp.dst, in0=src, scalar=grp.more["gate"], in1=grp.dst,
                                               op0=ALU.mult, op1=ALU.add).then_inc(proj_ev["D"], 1)
                    elif grp.kind == "times":
                        d.wait_ge(proj_ev["A"], self.nth[g - grp.more["back"]])
                        d.tensor_tensor(grp.dst, src, self.half[:, halves % 4, 0:n],
                                        ALU.mult).then_inc(proj_ev["D"], 1)
                        halves += 1

        def chunks(context=True):
            out = [(0, 0, 512), (0, 512, 512)]
            return out + [(1, 0, 256)] if context else out

        h_of, y_of, x_of = (h_l, h_c), (y_l, y_c), (x_l, x_c)

        G_U = mem(STAGE, 4, S + L + 2 * (TAPS - 1))
        HALF = TAPS // 2
        u_at = (HALF, S + 3 * HALF)
        tmp4 = mem(STAGE + 2 * 4096 - 0, 4, 512)
        assert 4 * (S + L + 2 * (TAPS - 1)) == 5360

        p_ab_a = []
        for ct in range(4):
            for (w_, t0, n) in chunks():
                cols = (256 * ct, 256 * ct + 256)
                unit = ("ab_in", cols[0] // 512)
                c0 = cols[0] % 512
                p_ab_a.append(Group(unit, (c0, c0 + 128), ("ch", h_of[w_], t0, n), "sigmoid", None))
                p_ab_a.append(Group(unit, (c0 + 128, c0 + 256), ("ch", h_of[w_], t0, n), "times",
                                    G_U[:, ct, u_at[w_] + t0:u_at[w_] + t0 + n], back=1))
        P_AB_A = Projection(p_ab_a, 0, half=tmp4)
        kT = mem(STAGE + 5360, S + L)
        vv = mem(STAGE + 6640, 10, P)
        AB_TMP = STAGE + 7920
        g_ = []
        for ct in range(4):
            for i, (w_, t0, n) in enumerate(chunks()):
                g_.append(Group(("ab_in", 2), (128 * ct, 128 * ct + 128), ("ch", h_of[w_], t0, n),
                                "copyA" if i % 2 else "copyD", y_of[w_][:, 4 + ct, t0:t0 + n]))
        for i, (w_, t0, n) in enumerate(chunks()):
            g_.append(Group(("ab_in", 3), (0, 128), ("ch", h_of[w_], t0, n), "copyA" if i % 2 else "copyD",
                            kT[:, S * w_ + t0:S * w_ + t0 + n]))
        for i in range(10):
            g_.append(Group(("ab_in", 3), (128, 256), ("tok", h_of[i // 8], 128 * (i % 8), 128),
                            "copyA" if i % 2 else "copyD", vv[:, i]))
        P_AB_Q = Projection(g_, 0)

        def z_groups(name, j0, context):
            out = []
            for ct in range(KT):
                for (w_, t0, n) in chunks(context):
                    out.append(Group((name, j0 + ct // 4), (ct % 4 * 128, ct % 4 * 128 + 128),
                                     ("ch", h_of[w_], t0, n), "silu", y_of[w_][:, ct, t0:t0 + n]))
            return out

        def out_groups(name, m, tile0, context):
            out = []
            for ct in range(KT):
                for (w_, t0, n) in chunks(context):
                    out.append(Group((name, ct // 4), (ct % 4 * 128, ct % 4 * 128 + 128),
                                     ("ch", y_of[w_], t0, n), "resid", x_of[w_][:, ct, t0:t0 + n],
                                     gate=mod[m][:, tile0 + ct, w_:w_ + 1]))
            return out

        tmpz = mem(STAGE, 4, 512)
        P_AB_Z = Projection(z_groups("ab_in", 4, True), 0, half=tmpz)
        P_AB_O = Projection(out_groups("ab_out", "ab", 16, True), 0)

        g_ = []
        for ct in range(4):
            for i, (w_, t0, n) in enumerate(chunks(False)):
                g_.append(Group(("cd_in", 0), (128 * ct, 128 * ct + 128), ("ch", h_l, t0, n),
                                "copyA" if i % 2 else "copyD", y_l[:, ct, t0:t0 + n]))
        P_CD_F = Projection(g_, 0)
        kcd = mem(STAGE, 4, S + L)
        vcd = mem(STAGE + 4 * 1280, 10, 512)
        g_ = []
        for ct in range(4):
            for i, (w_, t0, n) in enumerate(chunks(False)):
                g_.append(Group(("cd_in", 1), (128 * ct, 128 * ct + 128), ("ch", h_l, t0, n),
                                "copyA" if i % 2 else "copyD", y_l[:, 4 + ct, t0:t0 + n]))
        for ct in range(4):
            for i, (w_, t0, n) in enumerate(chunks()):
                g_.append(Group(("cd_in", 2), (128 * ct, 128 * ct + 128), ("ch", h_of[w_], t0, n),
                                "copyA" if i % 2 else "copyD", kcd[:, ct, S * w_ + t0:S * w_ + t0 + n]))
        for i in range(10):
            g_.append(Group(("cd_in", 3), (0, 512), ("tok", h_of[i // 8], 128 * (i % 8), 512),
                            "copyA" if i % 2 else "copyD", vcd[:, i]))
        P_CD_Q = Projection(g_, 0)
        P_CD_Z = Projection(z_groups("cd_in", 4, False), 0, half=tmpz)
        P_CD_O = Projection(out_groups("cd_out", "cd", 16, False), 0)

        kev = mem(STAGE, S + L)
        vev = mem(STAGE + 1280, 10, P)
        zev = mem(STAGE + 2560, KT, 512)
        EV_TMP = STAGE + 2560 + 4096
        g_ = []
        for ct in range(4):
            for i, (w_, t0, n) in enumerate(chunks(False)):
                g_.append(Group(("ev_in", 0), (128 * ct, 128 * ct + 128), ("ch", h_l, t0, n), "copyD",
                                y_l[:, ct, t0:t0 + n]))
        for i, (w_, t0, n) in enumerate(chunks()):
            g_.append(Group(("ev_in", 1), (0, 128), ("ch", h_of[w_], t0, n), "copyD",
                            kev[:, S * w_ + t0:S * w_ + t0 + n]))
        for i in range(10):
            g_.append(Group(("ev_in", 1), (128, 256), ("tok", h_of[i // 8], 128 * (i % 8), 128), "copyD",
                            vev[:, i]))
        for ct in range(4):
            for (w_, t0, n) in chunks(False):
                g_.append(Group(("ev_in", 2), (128 * ct, 128 * ct + 128), ("ch", h_l, t0, n), "gelu",
                                y_l[:, 4 + ct, t0:t0 + n]))
        for i in range(8):
            g_.append(Group(("ev_in", 3), (0, 512), ("tok", h_l, 128 * i, 512), "gelu", zev[:, i]))
        P_EV = Projection(g_, 0)
        P_EV_O = Projection(out_groups("ev_out", "l0", 16, False), 0)

        g_ = []
        prod = mem(STAGE, KT, S + 2)
        gate_b = mem(YT, KT, S)
        for ct in range(KT):
            base = 3 * ct * 128
            for j, kind in ((0, "keep"), (1, "times"), (2, "copyA")):
                u_, c0 = (base + 128 * j) // 512, (base + 128 * j) % 512
                for (w_, t0, n) in chunks(False):
                    dst = prod[:, ct, 1 + t0:1 + t0 + n] if kind == "times" else gate_b[:, ct, t0:t0 + n]
                    g_.append(Group(("od_in", u_), (c0, c0 + 128), ("ch", h_l, t0, n), kind, dst, back=2))
        OD_TMP = STAGE + KT * (S + 2)
        P_OD = Projection(g_, 0, half=mem(OD_TMP, 4, 512))
        P_OD_O = Projection(out_groups("od_out", "l1", 16, False), 0)

        silu_c = mem(SILU, 32)
        mod_mm = sem("mod_mm")
        MODS = [("ab", "ab_ada", "ab_b_ada", 0), ("cd", "cd_ada", "cd_b_ada", 0), ("l0", "l0_ada", "b_ada0", 1),
                ("l1", "l1_ada", "b_ada1", 1)]

        def mod_bank(which):
            a_ = 128 + 2 * sum(NMOD[m[0]][0] for m in MODS[1:which])
            return bank(7)[:, a_:a_ + 2 * NMOD[MODS[which][0]][0]]

        def mod_units(which):
            return sum(NMOD[m[0]][0] // 4 for m in MODS[:which])

        for i, m_ in enumerate(MODS):
            for j in range(NMOD[m_[0]][0] // 4 if i == 0 else 0):
                unit_used[unit_no[(m_[1], j)]] = (mod_mm, mod_units(i) + j + 1)

        MOD_ITEMS = [(i, j, half, col) for i, j in [(1, j) for j in range(6)] + [(2, j) for j in range(4)]
                     for half in range(2) for col in range(2)]
        PAIRED = len(MOD_ITEMS)
        MOD_ITEMS += [(i, j, None, 0) for i, j in [(2, j) for j in range(4, 12)] + [(3, j) for j in range(12)]]
        mod_v, mod_col = sem("mod_v"), sem("mod_col")
        mod_acc = mem(XC + 1280, 3, 256)
        mod_to = mem(STAGE + 3 * UNIT - 4, 3)
        mod_to_set = sem("mod_to_set")
        for n, (i, j, half, col) in enumerate(MOD_ITEMS):
            unit_used[unit_no[(MODS[i][1], j)]] = (mod_v, KT * (n + 1)) if n < PAIRED else (mod_col, n + 1)

        mod_at = [0]

        def mod_sum_dve(d):
            mod_at[0] = 0
            for n, (i, j, half, col) in enumerate(MOD_ITEMS):
                wts = unit_wait(d, MODS[i][1], j)
                if 3 <= n < PAIRED:
                    d.wait_ge(mod_col, n - 2 if n % 2 == 0 else n - 1)
                for k in range(KT):
                    at_ = 16 * MODS[i][3] + 2 * k + col
                    s_k = silu_c[:, at_:at_ + 1]
                    w_k = wts[:, k, 256 * half:256 * half + 256] if n < PAIRED else wts[:, k]
                    acc = mod_acc[:, n % 3] if n < PAIRED else wts[:, 0]
                    if k == 0:
                        d.tensor_scalar(acc, w_k, s_k, None, ALU.mult).then_inc(mod_v, 1)
                    else:
                        d.wait_ge(mod_v, KT * n + k)
                        d.scalar_tensor_tensor(out=acc, in0=w_k, scalar=s_k, in1=acc, op0=ALU.mult,
                                               op1=ALU.add).then_inc(mod_v, 1)
                    mod_at[0] += 1
                    yield

        def mod_col_pe(pe):
            for n, (i, j, half, col) in enumerate(MOD_ITEMS):
                if n >= PAIRED:
                    yield
                pe.wait_ge(mod_v, KT * (n + 1))
                if col == 1:
                    for h in range(2):
                        at_ = 2 * (4 * j + 2 * half + h)
                        for c_ in range(2):
                            last = pe.matmul(mod_bank(i)[:, at_:at_ + 2],
                                             mod_acc[:, (n - 1 + c_) % 3, 128 * h:128 * h + 128],
                                             mod_to[:, 1 - c_:3 - c_], start=c_ == 0, stop=c_ == 1)
                    last.then_inc(mod_col, 2)
                elif n >= PAIRED:
                    src = ring[:, unit_no[(MODS[i][1], j)] % 2, 0:512]
                    for h in range(4):
                        last = pe.matmul(mod_bank(i)[:, 2 * (4 * j + h):2 * (4 * j + h) + 2],
                                         src[:, 128 * h:128 * h + 128], ones[:, 0:2], start=True, stop=True)
                    last.then_inc(mod_col, 1)
                yield

        def mod_pe(pe, which):
            name, wname, _, blk = MODS[which]
            for ct in range(NMOD[name][0]):
                if ct % 4 == 0:
                    wts = unit_wait(pe, wname, ct // 4)
                for k in range(KT):
                    last = pe.matmul(mod_bank(which)[:, 2 * ct:2 * ct + 2], wts[:, k, ct % 4 * 128:ct % 4 * 128 + 128],
                                     silu_c[:, 16 * blk + 2 * k:16 * blk + 2 * k + 2], start=k == 0,
                                     stop=k == KT - 1)
                if ct % 4 == 3:
                    last.then_inc(mod_mm, 1)
                yield

        def mod_dve(d, link, which):
            name, _, bname, _ = MODS[which]
            n = NMOD[name][0]
            if which == 0:
                d.wait_ge(mod_mm, mod_units(1))
            else:
                d.wait_ge(mod_col, len(MOD_ITEMS))
            b = v(bname, 0, n).unsqueeze(2).broadcast_to([P, n, 2])
            link(d.tensor_tensor(mod[name], mod_bank(which).rearrange("p (a b) -> p a b", b=2), b, ALU.add))
            todo = [(name, 8, {"ab": "ab_norm_g", "cd": "cd_norm_g", "l0": "g_norm1_0", "l1": "g_norm1_1"}[name])]
            if n == 48:
                todo.append((name + "b", 32, {"l0": "g_norm2_0", "l1": "g_norm2_1"}[name]))
            for out, t0, g in todo:
                link(d.tensor_scalar(gs[out], mod[name][:, t0:t0 + 8], 1.0, None, ALU.add))
                link(d.tensor_tensor(gs[out], gs[out], v(g, 0, 8).unsqueeze(2).broadcast_to([P, 8, 2]), ALU.mult))

        nrm_sq, nrm_mm, nrm_rt, nrm_x, nrm_rc = (sem(s_) for s_ in ("nrm_sq", "nrm_mm", "nrm_rt", "nrm_x", "nrm_rc"))
        nrm_total = [0, 0]

        class Norm:
            def __init__(self, context, scale, shift, final=False):
                self.ch = chunks(context)
                self.scale, self.shift, self.final = scale, shift, final
                self.tiles0, self.ch0 = nrm_total
                nrm_total[0] += KT * len(self.ch)
                nrm_total[1] += len(self.ch)
                self.root = mem(words - 3 * 512, 3, 512)

            def act(self, a):
                for i, (w_, t0, n) in enumerate(self.ch):
                    for k in range(KT):
                        a.activation(h_of[w_][:, k, t0:t0 + n], x_of[w_][:, k, t0:t0 + n],
                                     ACT.Square).then_inc(nrm_sq, 1)
                for i, (w_, t0, n) in enumerate(self.ch):
                    a.wait_ge(nrm_mm, self.ch0 + i + 1)
                    a.activation(self.root[:, i, 0:n], bank(i)[:, 0:n], ACT.Sqrt, scale=1.0 / D,
                                 bias=eps).then_inc(nrm_rt, 1)
                for i, (w_, t0, n) in enumerate(self.ch):
                    for k in range(KT):
                        a.wait_ge(nrm_x, self.tiles0 + KT * i + k + 1)
                        if self.final:
                            a.activation(x_of[w_][:, k, t0:t0 + n], h_of[w_][:, k, t0:t0 + n], ACT.Copy,
                                         scale=self.scale(k, w_))
                        else:
                            a.activation(h_of[w_][:, k, t0:t0 + n], h_of[w_][:, k, t0:t0 + n], ACT.Identity,
                                         scale=self.scale(k, w_), bias=self.shift(k, w_))

            def pe(self, pe):
                for i, (w_, t0, n) in enumerate(self.ch):
                    for k in range(KT):
                        pe.wait_ge(nrm_sq, self.tiles0 + KT * i + k + 1)
                        last = pe.matmul(bank(i)[:, 0:n], ones, h_of[w_][:, k, t0:t0 + n], start=k == 0,
                                         stop=k == KT - 1)
                    last.then_inc(nrm_mm, 1)

            def dve(self, d):
                for i, (w_, t0, n) in enumerate(self.ch):
                    d.wait_ge(nrm_rt, self.ch0 + i + 1)
                    d.reciprocal(self.root[:, i, 0:n], self.root[:, i, 0:n]).then_inc(nrm_rc, 1)
                    d.wait_ge(nrm_rc, self.ch0 + i + 1)
                    for k in range(KT):
                        d.tensor_tensor(h_of[w_][:, k, t0:t0 + n], x_of[w_][:, k, t0:t0 + n],
                                        self.root[:, i, 0:n], ALU.mult).then_inc(nrm_x, 1)

        def norm_of(name, m, shift_at, context, w_out_c=None):
            return Norm(context, lambda k, w_: gs[name][:, k, w_:w_ + 1],
                        lambda k, w_: mod[m][:, shift_at + k, w_:w_ + 1])

        N_AB = norm_of("ab", "ab", 0, True)
        N_CD = norm_of("cd", "cd", 0, True)
        N_F1 = Norm(False, lambda k, w_: v("final_g", k), None, final=True)
        N_L0 = norm_of("l0", "l0", 0, True)
        N_L0B = norm_of("l0b", "l0", 24, False)
        N_L1 = norm_of("l1", "l1", 0, False)
        N_L1B = norm_of("l1b", "l1", 24, False)
        N_F2 = Norm(False, lambda k, w_: v("g_final2", k), None, final=True)

        conv_n = sem("conv_n")
        ln_sq, ln_mm, ln_rt, ln_x, ln_c = (sem(s_) for s_ in ("ln_sq", "ln_mm", "ln_rt", "ln_x", "ln_c"))
        ln_root = mem(STAGE, 3, 512)

        def conv_dve(d):
            n = 0
            for tap in range(TAPS):
                for ct in range(4):
                    for w_, T in ((0, S), (1, L)):
                        out = y_of[w_][:, ct, 0:T]
                        a0 = u_at[w_] - HALF + tap
                        src = G_U[:, ct, a0:a0 + T]
                        wt = v("ab_conv_w", ct * TAPS + tap)
                        if tap == 0:
                            d.tensor_scalar(out, src, wt, v("ab_conv_b", ct), ALU.mult, ALU.add).then_inc(conv_n, 1)
                        else:
                            d.wait_ge(conv_n, n - 7)
                            d.scalar_tensor_tensor(out=out, in0=src, scalar=wt, in1=out, op0=ALU.mult,
                                                   op1=ALU.add).then_inc(conv_n, 1)
                        n += 1
                        yield

        def conv_and_mods(d):
            mods, conv = mod_sum_dve(d), conv_dve(d)
            while True:
                for _ in range(KT if mod_at[0] < PAIRED * KT else KT // 2):
                    next(mods, None)
                for _ in range(3 if mod_at[0] <= PAIRED * KT else 4):
                    if next(conv, conv) is conv and mod_at[0] == KT * len(MOD_ITEMS):
                        return
                yield

        def ln_pe(pe):
            for i, (w_, t0, n) in enumerate(chunks()):
                for k in range(4):
                    last = pe.matmul(bank(i)[:, 0:n], ones, y_of[w_][:, k, t0:t0 + n], start=k == 0, stop=k == 3)
                last.then_inc(ln_mm, 1)
            for i, (w_, t0, n) in enumerate(chunks()):
                for k in range(4):
                    pe.wait_ge(ln_sq, 4 * i + k + 1)
                    last = pe.matmul(bank(3 + i)[:, 0:n], ones, ln_sqr[w_][:, k, t0:t0 + n], start=k == 0,
                                     stop=k == 3)
                last.then_inc(ln_mm, 1)

        ln_sqr = (mem(STAGE + 1536, 4, S), mem(STAGE + 1536 + 4 * S, 4, L))

        def ln_dve(d):
            for i, (w_, t0, n) in enumerate(chunks()):
                d.wait_ge(ln_mm, i + 1)
                for k in range(4):
                    y = y_of[w_][:, k, t0:t0 + n]
                    d.scalar_tensor_tensor(out=y, in0=bank(i)[:, 0:n], scalar=-1.0 / 512, in1=y, op0=ALU.mult,
                                           op1=ALU.add).then_inc(ln_c, 1)
            for i, (w_, t0, n) in enumerate(chunks()):
                d.wait_ge(ln_rt, i + 1)
                r = ln_root[:, i, 0:n]
                d.reciprocal(r, r).then_inc(ln_x, 1)
                d.wait_ge(ln_x, 5 * i + 1)
                for k in range(4):
                    y = y_of[w_][:, k, t0:t0 + n]
                    d.scalar_tensor_tensor(out=y, in0=y, scalar=v("ab_ln_g", k), in1=r, op0=ALU.mult,
                                           op1=ALU.mult).then_inc(ln_x, 1)

        def ln_act(a):
            for i, (w_, t0, n) in enumerate(chunks()):
                for k in range(4):
                    a.wait_ge(ln_c, 4 * i + k + 1)
                    a.activation(ln_sqr[w_][:, k, t0:t0 + n], y_of[w_][:, k, t0:t0 + n],
                                 ACT.Square).then_inc(ln_sq, 1)
            for i, (w_, t0, n) in enumerate(chunks()):
                a.wait_ge(ln_mm, 3 + i + 1)
                a.activation(ln_root[:, i, 0:n], bank(3 + i)[:, 0:n], ACT.Sqrt, scale=1.0 / 512,
                             bias=eps).then_inc(ln_rt, 1)
            for i, (w_, t0, n) in enumerate(chunks()):
                for k in range(4):
                    a.wait_ge(ln_x, 5 * i + k + 2)
                    y = y_of[w_][:, k, t0:t0 + n]
                    a.activation(y, y, ACT.Silu, bias=v("ab_ln_b", k))

        hd_ld, hd_sq, hd_mm, hd_rt, hd_q, hd_sw, hd_done = (
            sem(s_) for s_ in ("hd_ld", "hd_sq", "hd_mm", "hd_rt", "hd_q", "hd_sw", "hd_done"))
        rope = mem(XC, 2, S)
        hd_tmp = mem(AB_TMP, 2, 1280)

        ab_heads = [(y_l[:, 4 + i], y_c[:, 4 + i], "ab_qn_g") for i in range(4)] + \
                   [(kT[:, 0:S], kT[:, S:S + L], "ab_kn_g")]

        def pieces(i):
            a, b, _ = ab_heads[i]
            return [(a[:, 0:512], 0, 512), (a[:, 512:1024], 512, 512), (b, 1024, 256)]

        def hd_act(a):
            for i in range(5):
                for j, (q, t0, n) in enumerate(pieces(i)):
                    if i:
                        a.wait_ge(hd_done, i)
                    a.activation(hd_tmp[:, 0, t0:t0 + n], q, ACT.Square).then_inc(hd_sq, 1)
                for j, (q, t0, n) in enumerate(pieces(i)):
                    a.wait_ge(hd_mm, 3 * i + j + 1)
                    a.activation(hd_tmp[:, 1, t0:t0 + n], bank(j)[:, 0:n], ACT.Sqrt, scale=1.0 / HEAD,
                                 bias=eps).then_inc(hd_rt, 1)

        def hd_pe(pe):
            for i in range(5):
                for j, (q, t0, n) in enumerate(pieces(i)):
                    pe.wait_ge(hd_sq, 3 * i + j + 1)
                    pe.matmul(bank(j)[:, 0:n], c("head_ones"), hd_tmp[:, 0, t0:t0 + n], start=True,
                              stop=True).then_inc(hd_mm, 1)
                for j, (q, t0, n) in enumerate(pieces(i)[:2]):
                    pe.wait_ge(hd_q, 2 * 3 * i + 2 * j + 2)
                    pe.matmul(bank(3 + j), c("swap_ab"), q, start=True, stop=True).then_inc(hd_sw, 1)

        def hd_dve(d, link):
            d.wait_ge(hd_ld, 16)
            for i in range(5):
                g = v(ab_heads[i][2])
                for j, (q, t0, n) in enumerate(pieces(i)):
                    r = hd_tmp[:, 1, t0:t0 + n]
                    d.wait_ge(hd_rt, 3 * i + j + 1)
                    d.reciprocal(r, r).then_inc(hd_q, 1)
                    d.wait_ge(hd_q, 2 * (3 * i + j) + 1)
                    d.scalar_tensor_tensor(out=q, in0=q, scalar=g, in1=r, op0=ALU.mult,
                                           op1=ALU.mult).then_inc(hd_q, 1)
                d.wait_ge(hd_q, 6 * (i + 1))
                for j, (q, t0, n) in enumerate(pieces(i)[:2]):
                    d.wait_ge(hd_sw, 2 * i + j + 1)
                    s_ = hd_tmp[:, 0, t0:t0 + n]
                    link(d.tensor_tensor(s_, bank(3 + j), rope[:, 1, t0:t0 + n], ALU.mult))
                    link(d.tensor_tensor(q, q, rope[:, 0, t0:t0 + n], ALU.mult))
                    link(d.tensor_tensor(q, q, s_, ALU.add))
                d.sem_inc(hd_done, 1)

        ev_ld, ev_sw, ev_done = sem("ev_ld"), sem("ev_sw"), sem("ev_done")
        rope_e = mem(EV_TMP, 2, S)
        ev_tmp = mem(EV_TMP + 2048, 512)
        ev_heads = [y_l[:, i] for i in range(4)] + [kev[:, 0:S]]

        def rope_pe(pe):
            for i in range(5):
                for j in range(2):
                    if i:
                        pe.wait_ge(ev_done, 2 * (i - 1) + j + 1)
                    pe.matmul(bank(j), c("swap_ev"), ev_heads[i][:, 512 * j:512 * j + 512], start=True,
                              stop=True).then_inc(ev_sw, 1)

        def rope_dve(d, link):
            d.wait_ge(ev_ld, 16)
            for i in range(5):
                for j in range(2):
                    t0 = 512 * j
                    q = ev_heads[i][:, t0:t0 + 512]
                    d.wait_ge(ev_sw, 2 * i + j + 1)
                    link(d.tensor_tensor(ev_tmp, bank(j), rope_e[:, 1, t0:t0 + 512], ALU.mult))
                    link(d.tensor_tensor(q, q, rope_e[:, 0, t0:t0 + 512], ALU.mult))
                    link(d.tensor_tensor(q, q, ev_tmp, ALU.add))
                    d.sem_inc(ev_done, 1)

        s_ready, mx_ready, p_ready = sem("s_ready"), sem("mx_ready"), sem("p_ready")
        pt_ready = sem("pt_ready")
        pt_ev = [sem("pt_ev_dve"), sem("pt_ev_act")]
        pv_done = sem("pv_done")
        o_norm = sem("o_norm")
        ot_ready, ot_done = sem("ot_ready"), sem("ot_done")
        att_total = {"units": 0, "groups": [0, 0], "tiles": 0}

        class Attention:
            def __init__(self, units_, s_words, p_words, p_at, pt_at, n_pt, o_at, pad, pe_fill=False, dve_fill=0):
                self.u = units_
                self.pad = pad
                self.wide = s_words > 1024
                self.s_banks = 3 if self.wide else 2
                self.turn_lag = 4 if self.wide else 3
                self.P = [mem(a_, p_words) for a_ in p_at]
                self.n_pt = n_pt
                self.PT = mem(pt_at, n_pt, 512)
                self.pe_fill, self.dve_fill = pe_fill, dve_fill
                self.O = mem(o_at, 2, 128)
                self.groups = []
                self.of_unit = []
                for i, un in enumerate(units_):
                    mine = [un["chunks"][j:j + 4] for j in range(0, len(un["chunks"]), 4)]
                    self.of_unit.append([len(self.groups) + j for j in range(len(mine))])
                    self.groups += mine
                self.tile_of = []
                n = 0
                for un in units_:
                    self.tile_of.append(n)
                    if un["full"] or un["side"] == 1:
                        n += 1
                self.u0, self.g0, self.t0 = att_total["units"], list(att_total["groups"]), att_total["tiles"]
                att_total["units"] += len(units_)
                att_total["groups"][0] += (len(self.groups) + 1) // 2
                att_total["groups"][1] += len(self.groups) // 2
                att_total["tiles"] += n

            def units_done(self, n):
                return self.u0 + n

            def groups_done(self, n):
                return sum(self.g0) + n

            def copies_done(self, g):
                return self.g0[g % 2] + g // 2 + 1

            def tiles_done(self, n):
                return self.t0 + n

            def scores(self, i):
                return bank(self.s_banks * (i % 2), self.s_banks)

            def tbank(self, g):
                return bank(6 if self.wide else 5 + g % 2)

            def obank(self, i):
                return bank(7)[:, 0:128]

            def ends_tile(self, i):
                return 0 <= i < len(self.u) and (self.u[i]["full"] or self.u[i]["side"] == 1)

            def turned(self, tile, i):
                return bank(3 * (i % 2) + 2)[:, 256:384] if self.wide else bank(4)[:, 0:128]

            def pe(self, pe, fill=iter(())):
                for i in range(len(self.u) + 4):
                    turn = i - self.turn_lag
                    if i < len(self.u):
                        un = self.u[i]
                        sc = self.scores(i)
                        if i >= 2:
                            pe.wait_ge(p_ready, self.units_done(i - 1))
                        if self.wide and self.ends_tile(turn):
                            self.out_turn(pe, turn, i)
                        for (r0, r1, c0, q, k) in un["scores"]:
                            if self.wide and self.ends_tile(turn) and c0 == 1024:
                                pe.wait_ge(ot_done, self.tiles_done(self.tile_of[turn] + 1))
                            last = pe.matmul(sc[r0:r1, c0:c0 + k.shape[1]], q, k, start=True, stop=True)
                        last.then_inc(s_ready, 1)
                    elif self.wide and self.ends_tile(turn):
                        self.out_turn(pe, turn, i)
                    if 2 <= i < len(self.u) + 2:
                        self.weigh(pe, i - 2, fill)
                    if not self.wide and self.ends_tile(turn):
                        self.out_turn(pe, turn, i)
                if self.pe_fill:
                    pe.wait_ge(o_norm, self.units_done(len(self.u)))
                for _ in fill:
                    pass

            def weigh(self, pe, i, fill):
                pb = self.P[i % 3]
                pe.wait_ge(p_ready, self.units_done(i + 1))
                mine = self.of_unit[i]

                def turn(g):
                    before = g - 1 if self.wide else g - 2
                    if before >= 0:
                        pe.wait_ge(pt_ev[before % 2], self.copies_done(before))
                    for j, (c0, K, V) in enumerate(self.groups[g]):
                        last = pe.transpose(self.tbank(g)[0:K, 128 * j:128 * j + 128], pb[:, c0:c0 + K], ident)
                    last.then_inc(pt_ready, 1)

                def values(g):
                    pe.wait_ge(pt_ev[g % 2], self.copies_done(g))
                    if g == mine[0] and i >= 1:
                        pe.wait_ge(o_norm, self.units_done(i))
                    for j, (c0, K, V) in enumerate(self.groups[g]):
                        last = pe.matmul(bank(7)[:, 0:V.shape[1]], self.PT[0:K, g % self.n_pt, 128 * j:128 * j + 128],
                                         V, start=g == mine[0] and j == 0,
                                         stop=g == mine[-1] and j == len(self.groups[g]) - 1)
                    last.then_inc(pv_done, 1)

                turn(mine[0])
                for g in mine[1:] + [None]:
                    if g is not None:
                        turn(g)
                    if self.pe_fill and g == (mine + [None])[1]:
                        if i >= 1:
                            pe.wait_ge(o_norm, self.units_done(i))
                        next(fill, None)
                    if g is not None:
                        values(g - 1)
                values(mine[-1])

            def out_turn(self, pe, i, slot):
                tile = self.tile_of[i]
                pe.wait_ge(o_norm, self.units_done(i + 1))
                if tile >= 1:
                    pe.wait_ge(ot_done, self.tiles_done(tile))
                pe.transpose(self.turned(tile, slot), self.O[:, tile % 2], ident).then_inc(ot_ready, 1)

            def dve(self, d, link, fill=iter(())):
                if self.pad:
                    for p in self.P:
                        link(d.memset(p[:, 0:self.pad], 0.0))
                for i in range(len(self.u) + 2):
                    copies = [g for g in self.of_unit[i - 2] if g % 2 == 0] if i >= 2 else []
                    for g in copies[:1]:
                        self.copy(d, g, 0)
                    if i < len(self.u):
                        self.maximum(d, link, i)
                    for g in copies[1:]:
                        self.copy(d, g, 0)
                    for _ in range(self.dve_fill):
                        next(fill, None)
                    if i >= 2:
                        self.divide(d, link, i - 2)
                for _ in fill:
                    pass

            def maximum(self, d, link, i):
                un, sc, pb, st = self.u[i], self.scores(i), self.P[i % 3], stat[:, i % 4]
                d.wait_ge(s_ready, self.units_done(i + 1))
                if i >= 4:
                    d.wait_ge(o_norm, self.units_done(i - 3))
                if un["add"]:
                    if i >= 3:
                        d.wait_ge(pt_ready, self.groups_done(self.of_unit[i - 3][-1] + 1))
                    for (c0, m, b) in un["add"]:
                        o = pb[:, self.pad + c0:self.pad + c0 + m]
                        if b is None:
                            last = d.tensor_scalar(o, sc[:, c0:c0 + m], SCALE, None, ALU.mult)
                        else:
                            last = d.scalar_tensor_tensor(out=o, in0=sc[:, c0:c0 + m], scalar=SCALE, in1=b,
                                                          op0=ALU.mult, op1=ALU.add)
                    link(last)
                    src, scale = pb[:, self.pad:self.pad + un["n"]], -1.0
                else:
                    src, scale = sc[:, 0:un["n"]], -SCALE
                link(d.tensor_reduce(st[:, 0:1], src, X_AXIS, ALU.max))
                if un["sink"] is not None:
                    link(d.tensor_tensor(st[:, 0:1], st[:, 0:1], un["sink"], ALU.max))
                d.tensor_scalar(st[:, 1:2], st[:, 0:1], scale, None, ALU.mult).then_inc(mx_ready, 1)

            def divide(self, d, link, i):
                un, st = self.u[i], stat[:, i % 4]
                d.wait_ge(p_ready, self.units_done(i + 1))
                if un["sink"] is not None:
                    link(d.tensor_tensor(st[:, 2:3], st[:, 2:3], st[:, 3:4], ALU.add))
                link(d.reciprocal(st[:, 4:5], st[:, 2:3]))
                d.wait_ge(pv_done, self.groups_done(self.of_unit[i][-1] + 1))
                tile = self.tile_of[i]
                if tile >= 2:
                    d.wait_ge(ot_ready, self.tiles_done(tile - 1))
                o = self.O[:, tile % 2] if un["full"] else self.O[:, tile % 2, 64 * un["side"]:64 * un["side"] + 64]
                d.tensor_scalar(o, bank(7)[:, 0:o.shape[1]], st[:, 4:5], None, ALU.mult).then_inc(o_norm, 1)

            def copy(self, eng, g, which):
                eng.wait_ge(pt_ready, self.groups_done(g + 1))
                if g >= self.n_pt:
                    eng.wait_ge(pv_done, self.groups_done(g - self.n_pt + 1))
                grp = self.groups[g]
                full = [j for j, x in enumerate(grp) if x[1] == P]
                parts = [(P, 0, 128 * len(full))] if full else []
                parts += [(x[1], 128 * j, 128 * j + 128) for j, x in enumerate(grp) if x[1] < P]
                for K, a, b in parts:
                    o, s_ = self.PT[0:K, g % self.n_pt, a:b], self.tbank(g)[0:K, a:b]
                    last = eng.tensor_copy(o, s_) if which == 0 else eng.activation(o, s_, ACT.Copy)
                last.then_inc(pt_ev[which], 1)

            def act(self, a):
                for i in range(len(self.u) + 4):
                    turn = i - self.turn_lag
                    if self.wide and self.ends_tile(turn):
                        self.write(a, turn, i)
                    if 2 <= i < len(self.u) + 2:
                        for g in self.of_unit[i - 2]:
                            if g % 2 == 1:
                                self.copy(a, g, 1)
                    if i < len(self.u):
                        un, st = self.u[i], stat[:, i % 4]
                        pb, n = self.P[i % 3], un["n"]
                        a.wait_ge(mx_ready, self.units_done(i + 1))
                        if i >= 4:
                            a.wait_ge(o_norm, self.units_done(i - 3))
                        if un["add"]:
                            src, scale = pb[:, self.pad:self.pad + n], 1.0
                        else:
                            src, scale = self.scores(i)[:, 0:n], SCALE
                            if i >= 3:
                                a.wait_ge(pt_ready, self.groups_done(self.of_unit[i - 3][-1] + 1))
                        if un["sink"] is not None:
                            a.activation(st[:, 3:4], un["sink"], ACT.Exp, bias=st[:, 1:2])
                        a.activation(pb[:, self.pad:self.pad + n], src, ACT.Exp, bias=st[:, 1:2], scale=scale,
                                     accum_out=st[:, 2:3]).then_inc(p_ready, 1)
                    if not self.wide and self.ends_tile(turn):
                        self.write(a, turn, i)

            def write(self, a, i, slot):
                tile = self.tile_of[i]
                a.wait_ge(ot_ready, self.tiles_done(tile + 1))
                src = self.turned(tile, slot)
                for (r0, r1, c0, c1, dst) in self.u[i]["dst"]:
                    last = a.activation(dst, src[r0:r1, c0:c1], ACT.Copy)
                last.then_inc(ot_done, 1)

        us = []
        for qb in range(10):
            w_, q0 = qb // 8, 128 * (qb % 8)
            for ct in range(4):
                for side in range(2):
                    r = slice(64 * side, 64 * side + 64)
                    q = y_of[w_][r, 4 + ct, q0:q0 + 128]
                    k0 = 0 if w_ == 0 else S
                    nk = S + L - k0
                    sc, c0 = [], 0
                    while c0 < nk:
                        n = min(512, nk - c0)
                        sc.append((0, 128, c0, q, kT[r, k0 + c0:k0 + c0 + n]))
                        c0 += n
                    ch = [(128 * j, P, vv[:, k0 // 128 + j, r]) for j in range(nk // 128)]
                    us.append(dict(scores=sc, n=nk, s0=0, add=None, sink=None, chunks=ch, full=False, side=side,
                                   dst=[(0, 128, 0, 128, y_of[w_][:, 4 + ct, q0:q0 + 128])]))
        A_AB = Attention(us, 1280, 1280, (AB_TMP, AB_TMP + 1280, XC), AB_TMP + 2560, 3, AB_TMP + 4096, 0, pe_fill=True,
                         dve_fill=1)

        bias_at = YC
        bias = mem(YC, 4, RPB_R, GRID)
        us = []
        for r_ in range(ROWS):
            rs = min(max(r_ - NA_ROWS // 2, 0), ROWS - NA_ROWS)
            for pr in range(4):
                sc = []
                for side in range(2):
                    r = slice(64 * side, 64 * side + 64)
                    q = y_l[r, 4 + pr, GRID * r_:GRID * r_ + GRID]
                    sc.append((64 * side, 64 * side + 64, 0, q, kcd[r, pr, GRID * rs:GRID * rs + 512]))
                    sc.append((64 * side, 64 * side + 64, 512, q, kcd[r, pr, S:S + L]))
                cols = slice(128 * pr, 128 * pr + 128)
                if rs % 2 == 0:
                    ch = [(64 + 128 * j, P, vcd[:, rs // 2 + j, cols]) for j in range(4)]
                else:
                    ch = [(128 * j, P, vcd[:, rs // 2 + j, cols]) for j in range(4)]
                    ch.append((512, 64, vcd[0:64, rs // 2 + 4, cols]))
                ch += [(64 + 512 + 128 * j, P, vcd[:, 8 + j, cols]) for j in range(2)]
                ch.sort(key=lambda x: x[1] < P)
                d0 = rs - r_ + NA_ROWS - 1
                us.append(dict(scores=sc, n=768, s0=0, sink=None, chunks=ch, full=True, side=0,
                               add=[(0, 512, bias[:, pr, d0:d0 + NA_ROWS].rearrange("p a b -> p (a b)")),
                                    (512, 256, None)],
                               dst=[(0, 64, 0, 64, y_l[0:64, 4 + pr, GRID * r_:GRID * r_ + GRID]),
                                    (64, 128, 64, 128, y_l[64:128, 4 + pr, GRID * r_:GRID * r_ + GRID])]))
        A_CD = Attention(us, 1024, 832, (STAGE + 10240, STAGE + 10240 + 832, HC), HC + 832, 2, STAGE + 10240 + 1664, 64)

        wmask = mem(EV_TMP, 768)
        sinkc = mem(EV_TMP + 768, 8)
        us = []
        for qb in range(8):
            for ct in range(4):
                for side in range(2):
                    r = slice(64 * side, 64 * side + 64)
                    q = y_l[r, ct, 128 * qb:128 * qb + 128]
                    keys = ([(kev[r, 128 * (qb - 1):128 * qb], [qb - 1])] if qb else []) + \
                           [(kev[r, S:S + L], [8, 9])] + \
                           [(kev[r, 128 * qb:128 * qb + 128], [qb])] + \
                           ([(kev[r, 128 * qb + 128:128 * qb + 256], [qb + 1])] if qb < 7 else [])
                    sc, ch, c0 = [], [], 0
                    for k, tiles in keys:
                        n = k.shape[1]
                        sc.append((0, 128, c0, q, k))
                        for j, tl in enumerate(tiles):
                            ch.append((c0 + 128 * j, P, vev[:, tl, r]))
                        c0 += n
                    m0 = 0 if qb else 128
                    us.append(dict(scores=sc, n=c0, s0=0, sink=sinkc[:, ct + 4 * side:ct + 4 * side + 1], chunks=ch,
                                   full=False, side=side, add=[(0, c0, wmask[:, m0:m0 + c0])],
                                   dst=[(0, 128, 0, 128, y_l[:, ct, 128 * qb:128 * qb + 128])]))
        A_EV = Attention(us, 1024, 640, [EV_TMP + 776 + 640 * i for i in range(3)], EV_TMP + 776 + 1920, 4,
                         EV_TMP + 776 + 3968, 0)

        f_ld, f_ab, f_abe, f_t, f_te, f_y, f_ye = (sem(s_) for s_ in ("f_ld", "f_ab", "f_abe", "f_t", "f_te", "f_y", "f_ye"))
        f_mat = mem(STAGE, 2, 128)
        f_w = mem(STAGE + 256, 4, 128)
        f_m = mem(STAGE + 768, 2, 512)
        f_T = (mem(STAGE + 1792, KT, 512), mem(STAGE + 1792 + 4096, KT, 512))
        hank = mem(STAGE + 1792 + 8192, RPB_R * GRID)
        m_na = mem(STAGE + 1792 + 8192 + RPB_R * GRID, GRID)

        for j in range(4):
            unit_used[unit_no[("four", j)]] = (f_y, 4 * (j // 2) + 4)

        def four_pe(pe):
            pe.wait_ge(f_ld, 32)
            for j in range(2):
                for g in range(4):
                    last = pe.matmul(bank(j)[:, 128 * g:128 * g + 128], f_mat[:, j], f_w[:, g], start=True, stop=True)
                last.then_inc(f_ab, 1)
            for j in range(2):
                pe.wait_ge(f_abe, j + 1)
            for i in range(KT):
                for j in range(2):
                    n = 2 * i + j
                    if n >= 4:
                        pe.wait_ge(f_te, n - 3)
                    for g in range(4):
                        last = pe.matmul(bank(2 + n % 4)[:, 128 * g:128 * g + 128], y_l[:, g, 128 * i:128 * i + 128],
                                         f_m[:, j, 128 * g:128 * g + 128], start=True, stop=True)
                    last.then_inc(f_t, 1)
            pe.wait_ge(f_te, 2 * KT)
            for half in range(2):
                wts = [unit_wait(pe, "four", 2 * half), unit_wait(pe, "four", 2 * half + 1)]
                for g in range(4):
                    n = 4 * half + g
                    if n >= 4:
                        pe.wait_ge(f_ye, n - 3)
                    b_ = (0, 1, 6, 7)[n % 4]
                    for j in range(2):
                        for k in range(KT):
                            last = pe.matmul(bank(b_), f_T[j][:, k, 128 * g:128 * g + 128], wts[j][:, k],
                                             start=j == 0 and k == 0, stop=j == 1 and k == KT - 1)
                    last.then_inc(f_y, 1)

        def four_dve(d, link):
            d.wait_ge(f_ab, 1)
            d.tensor_copy(f_m[:, 0], bank(0)).then_inc(f_abe, 1)
            d.wait_ge(f_ab, 2)
            d.tensor_scalar(f_m[:, 1], bank(1), -1.0, None, ALU.mult).then_inc(f_abe, 1)
            for n in range(2 * KT):
                d.wait_ge(f_t, n + 1)
                d.tensor_copy(f_T[n % 2][:, n // 2], bank(2 + n % 4)).then_inc(f_te, 1)
            for pr in range(4):
                d.wait_ge(nb_ld, 16 * (3 + 2 * pr))
                src = hank.rearrange("p (a b) -> p a b", a=RPB_R)[:, :, ::-1]
                m = m_na.unsqueeze(1).broadcast_to([P, RPB_R, GRID])
                link(d.tensor_tensor(bias[:, pr], src, m, ALU.add))
                d.sem_inc(nb_use, 1)

        nb_ld, nb_use = sem("nb_ld"), sem("nb_use")

        def four_pool(g):
            g.dma_start(m_na, t["na_mask"]).then_inc(nb_ld, 16)
            for pr in range(4):
                if pr:
                    g.wait_ge(nb_use, pr)
                for side in range(2):
                    src = bass.AP(t["rpb_pad"].tensor, (2 * pr + side) * RPB_R * 127,
                                  [[1, GRID], [127, RPB_R], [1, GRID]])
                    g.dma_start(hank[64 * side:64 * side + 64].rearrange("p (a b) -> p a b", a=RPB_R),
                                src).then_inc(nb_ld, 16)

        def four_act(a):
            a.dma_start(f_mat, t["four_ch"].rearrange("p (a b) -> p a b", a=2)).then_inc(f_ld, 16)
            a.dma_start(f_w, t["w_four"].rearrange("g c e -> c g e")).then_inc(f_ld, 16)
            for n in range(8):
                a.wait_ge(f_y, n + 1)
                a.activation(y_l[:, n % 4, 512 * (n // 4):512 * (n // 4) + 512], bank((0, 1, 6, 7)[n % 4]),
                             ACT.Copy).then_inc(f_ye, 1)

        g_ld, g_sum, g_c, g_sq, g_z, g_b, g_mm, g_ev = (
            sem(s_) for s_ in ("g_ld", "g_sum", "g_c", "g_sq", "g_z", "g_b", "g_mm", "g_ev"))
        G0 = EV_TMP
        w_sp = mem(G0, 8, 128)
        b_sp = mem(G0 + 1024, 128, n=8)
        e_sp = mem(G0 + 1152, 4, 128, n=8)
        g_row = mem(G0 + 1664, 512)
        b_full = mem(G0 + 2176, 4, 128)
        z_sq = mem(G0 + 2688, 512)
        z_st = mem(G0 + 3200, 8, 4)
        s_tmp = mem(G0 + 3232, 2, 512)

        def sgu_act(a):
            for j in range(8):
                if j:
                    a.wait_ge(g_sum, j)
                a.activation(z_sq, zev[:, j], ACT.Copy, accum_out=z_st[:, j, 0:1]).then_inc(g_sum, 1)
            a.wait_ge(g_sum, 8)
            for j in range(8):
                a.wait_ge(g_c, 8 + j + 1)
                a.activation(z_sq, zev[:, j], ACT.Square, accum_out=z_st[:, j, 2:3]).then_inc(g_sq, 1)
                a.wait_ge(g_sq, j + 1)
            a.activation(z_st[:, :, 3], z_st[:, :, 2], ACT.Sqrt, scale=1.0 / 512, bias=eps).then_inc(g_sq, 1)

        def sgu_dve(d, link):
            for j in range(8):
                d.wait_ge(g_sum, j + 1)
                d.tensor_scalar(z_st[:, j, 1:2], z_st[:, j, 0:1], -1.0 / 512, None, ALU.mult).then_inc(g_c, 1)
            d.wait_ge(g_c, 8)
            for j in range(8):
                d.tensor_scalar(zev[:, j], zev[:, j], z_st[:, j, 1:2], None, ALU.add).then_inc(g_c, 1)
            d.wait_ge(g_sq, 9)
            link(d.reciprocal(z_st[:, :, 0], z_st[:, :, 3]))
            d.wait_ge(g_c, 16)
            d.wait_ge(g_ld, 64)
            for j in range(8):
                d.scalar_tensor_tensor(out=zev[:, j], in0=zev[:, j], scalar=z_st[:, j, 0:1], in1=g_row,
                                       op0=ALU.mult, op1=ALU.mult).then_inc(g_z, 1)
            d.wait_ge(g_b, 1)
            link(d.tensor_copy(b_full, bank(0).rearrange("p (a b) -> p a b", a=4)))
            for j in range(8):
                s_ = s_tmp[:, j % 2].rearrange("p (a b) -> p a b", a=4)
                u = y_l[:, 4:8, 128 * j:128 * j + 128]
                d.wait_ge(g_mm, j + 1)
                link(d.tensor_tensor(s_, bank(1 + j % 4).rearrange("p (a b) -> p a b", a=4), b_full, ALU.add))
                d.sem_inc(g_ev, 1)
                link(d.tensor_tensor(u, u, s_, ALU.mult))

        def sgu_pe(pe):
            pe.wait_ge(g_ld, 64)
            for hp in range(4):
                last = pe.matmul(bank(0)[:, 128 * hp:128 * hp + 128], e_sp[:, hp], b_sp, start=True, stop=True)
            last.then_inc(g_b, 1)
            for j in range(8):
                pe.wait_ge(g_z, j + 1)
                if j >= 4:
                    pe.wait_ge(g_ev, j - 3)
                for hp in range(4):
                    for side in range(2):
                        h = 2 * hp + side
                        last = pe.matmul(bank(1 + j % 4)[64 * side:64 * side + 64, 128 * hp:128 * hp + 128],
                                         zev[:, j, 64 * h:64 * h + 64], w_sp[:, h], start=True, stop=True,
                                         skip_group_check=True)
                last.then_inc(g_mm, 1)

        def sgu_pool(g):
            g.dma_start(w_sp, t["w_sp"].rearrange("j (h i) -> j h i", h=8)).then_inc(g_ld, 16)
            g.dma_start(b_sp, t["b_sp"]).then_inc(g_ld, 16)
            g.dma_start(e_sp, t["e_sp"].rearrange("h (a b) -> h a b", a=4)).then_inc(g_ld, 16)
            g.dma_start(g_row, t["g_sgu"].partition_broadcast(P)).then_inc(g_ld, 16)

        def conv3_dve(d, link):
            acc = mem(OD_TMP, 2, S)
            for ct in range(KT):
                a_ = acc[:, ct % 2]
                for tap in range(3):
                    wt = v("conv3_w", 3 * ct + tap)
                    src = prod[:, ct, tap:tap + S]
                    if tap == 0:
                        link(d.tensor_scalar(a_, src, wt, None, ALU.mult))
                    else:
                        link(d.scalar_tensor_tensor(out=a_, in0=src, scalar=wt, in1=a_, op0=ALU.mult, op1=ALU.add))
                link(d.tensor_tensor(gate_b[:, ct], gate_b[:, ct], a_, ALU.mult))

        M0 = STAGE
        rt_w = mem(M0, KT, 36)
        rt_b = mem(M0 + 288, 36)
        lg = mem(M0 + 324, 8, 36)
        r8 = [mem(M0 + 612 + 8 * i, 8) for i in range(10)]
        r32 = [mem(M0 + 700 + 32 * i, 8, 4) for i in range(3)]
        r64 = [mem(M0 + 800 + 64 * i, 8, 8) for i in range(5)]
        r256 = [mem(M0 + 1120 + 256 * i, 8, 32) for i in range(5)]
        cmp_n = mem(M0 + 2400, 32, S // BLK + 1, n=32)
        n_blk = mem(M0 + 2400 + 352, 128, n=32)
        ends = mem(M0 + 2400 + 480, 64)
        cmp_b = mem(M0 + 3000, NBLK, 32, n=1)
        tab_f = mem(M0 + 3000 + NBLK * 32, NBLK + 2, n=1)
        tok_id = mem(M0 + 4900, KT).bitcast(I32)
        zero_i = mem(M0 + 4910, NBLK).bitcast(I32)
        row_i = mem(M0 + 4964, BLK, n=NBLK).bitcast(I32)
        row_f = mem(M0 + 4964 + BLK, BLK, n=NBLK)
        h_tok = mem(M0 + 5300, 2, D)
        w_part = [[mem(a + i * UNIT, KT, 512) if i < 2 else mem(a + i * UNIT, 4, D) for i in range(3)]
                  for a in (YT, STAGE)]
        xb = mem(HT, 2, D)
        xbT = mem(HT + 2 * D, 2, KT, BLK)
        sg = mem(HT + 2 * D + 2 * KT * BLK, 2, 4 * BLK)
        hid = mem(HT + 2 * D + 2 * KT * BLK + 8 * BLK, 2, 4, BLK)
        y_sb = mem(HT + 2 * D + 2 * KT * BLK + 16 * BLK, 2, D)
        y_g = mem(HT, 4, D)
        y_s = mem(HT + 4 * D, 2, D)

        (m_ld, m_lg, m_tt, m_te, m_gx, m_ex, m_mk, m_rk, m_nb, m_pb, m_tab, m_zf, m_sc, m_cc, m_ct, m_cx) = (
            sem("moe_" + s_) for s_ in ("ld", "lg", "tt", "te", "gx", "ex", "mk", "rk", "nb", "pb", "tab",
                                        "zf", "sc", "cc", "ct", "cx"))

        m_zm = sem("moe_zm")
        m_ri, m_rf, m_rt = (sem("moe_" + s_) for s_ in ("ri", "rf", "rt"))
        m_tw = [sem("moe_tw0"), sem("moe_tw1")]
        m_cg = [sem("moe_cg0"), sem("moe_cg1")]

        class Moe:
            def __init__(self, l):
                self.l = l
                s = lambda x: sem(f"moe{l}_{x}")
                self.w_in = [[s(f"w_in{i}{j}") for j in range(3)] for i in range(2)]
                self.ix, self.xg = s("ix"), [s("xg0"), s("xg1")]
                self.xt, self.xe = s("xt"), s("xe")
                self.gg, self.gu = s("gg"), s("gu")
                self.sg, self.hid = s("sg"), s("hid")
                self.yd = s("yd")
                self.ye = [s("ye0"), s("ye1")]
                self.passed = s("passed")
                self.yw = [s("yw0"), s("yw1")]

            def route_pool(self, g):
                l = self.l
                g.dma_start(rt_w, t["w_router"][l].rearrange("(k p) n -> p k n", p=P)).then_inc(m_ld, 16)
                g.dma_start(rt_b, t["b_router"][l].partition_broadcast(P)).then_inc(m_ld, 16)
                g.dma_start(tok_id, t["tok_id"]).then_inc(m_ld, 16)
                g.memset(zero_i.bitcast(F32), 0.0).then_inc(m_zm, 1)
                g.wait_ge(m_zm, l + 1)
                g.dma_start(t["row_tok"].rearrange("(r b) o -> r (b o)", r=BLK),
                            zero_i[0:BLK]).then_inc(m_zf, 16)
                g.wait_ge(m_zf, 16 * l + 16)
                g.wait_ge(m_ld, 48 * (l + 1))
                g.wait_ge(m_tab, l + 1)
                for i in range(KT):
                    for a in range(2):
                        g.indirect_dma_start(t["row_tok"], bass.IndirectOffsetOnAxis(ap=moe_i[:, a, i:i + 1], axis=0),
                                             tok_id[:, i:i + 1], None).then_inc(m_sc, 16)
                g.wait_ge(m_sc, 256 * (l + 1))
                g.dma_start(row_i, t["row_tok"].rearrange("(b r) o -> b (r o)", r=BLK)).then_inc(m_ri, 16)

            def route_pe(self, pe):
                l = self.l
                pe.wait_ge(m_ld, 48 * (l + 1))
                for i in range(KT):
                    for k in range(KT):
                        last = pe.matmul(bank(0)[:, 36 * i:36 * i + 36], h_l[:, k, 128 * i:128 * i + 128],
                                         rt_w[:, k], start=k == 0, stop=k == KT - 1)
                last.then_inc(m_lg, 1)
                for i in range(KT):
                    if i >= 2:
                        pe.wait_ge(m_te, KT * l + i - 1)
                    b = bank(2 + 2 * (i % 2), 2)
                    for k in range(KT):
                        last = pe.transpose(b[:, 128 * k:128 * k + 128], h_l[:, k, 128 * i:128 * i + 128], ident)
                    last.then_inc(m_tt, 1)
                pe.wait_ge(m_mk, l + 1)
                mk = r256[2]
                for i in range(KT):
                    for j in range(i + 1):
                        last = pe.matmul(bank(1)[:, 32 * i:32 * i + 32], c("before") if j == i else ones, mk[:, j],
                                         start=j == 0, stop=j == i)
                for i in range(KT):
                    last = pe.matmul(bank(6)[0:32, 0:128], mk[:, i], ones, start=i == 0, stop=i == KT - 1)
                last.then_inc(m_rk, 1)
                pe.wait_ge(m_nb, l + 1)
                pe.matmul(bank(7)[:, 0:32], n_blk, c("expert_before", 32), start=True, stop=True)
                pe.matmul(bank(7)[:, 32:64], n_blk, c("expert_upto", 32), start=True,
                          stop=True).then_inc(m_pb, 1)
                pe.wait_ge(m_rf, l + 1)
                pe.transpose(bank(6)[0:BLK, 128:128 + NBLK], row_f, ident[0:NBLK, 0:NBLK]).then_inc(m_rt, 1)

            def route_act(self, a):
                l = self.l

                def exps(which, out, src):
                    a.wait_ge(m_gx, 2 * l + which)
                    a.activation(out, src, ACT.Exp).then_inc(m_ex, 1)

                for i in range(KT):
                    if i == 3:
                        exps(1, r32[1], r32[0])
                    if i == 6:
                        exps(2, r8[6], r8[5])
                    a.wait_ge(m_tt, KT * l + i + 1)
                    if i >= 2:
                        a.wait_ge(m_tw[i % 2], 16 * (KT // 2 * l + i // 2))
                    a.activation(h_tok[:, i % 2], bank(2 + 2 * (i % 2), 2), ACT.Copy).then_inc(m_te, 1)
                    a.wait_ge(m_te, KT * l + i + 1)
                    a.dma_start(t["h_tok"][128 * i:128 * i + 128, :], h_tok[:, i % 2]).then_inc(m_tw[i % 2], 16)
                for tw in m_tw:
                    a.wait_ge(tw, 16 * KT // 2 * (l + 1))

            def route_dve(self, d, link):
                l = self.l
                b8 = lambda x, n: x.unsqueeze(2).broadcast_to([P, 8, n])
                iota4 = c("iota4").unsqueeze(1).broadcast_to([P, 8, 4])
                iota8 = c("iota8").unsqueeze(1).broadcast_to([P, 8, 8])
                d.wait_ge(m_ld, 48 * (l + 1))
                d.wait_ge(m_lg, l + 1)
                link(d.tensor_tensor(lg, bank(0)[:, 0:288].rearrange("p (t n) -> p t n", n=36),
                                     rt_b.unsqueeze(1).broadcast_to([P, 8, 36]), ALU.add))
                g_max, g_sum, v1, v2, i_, dv, ev, p1, g_w, den = r8
                gd, ge, gm = r32
                first = lambda out, tmp, hit, iota, idx: (
                    link(d.tensor_scalar(tmp, hit, -64.0, None, ALU.mult)),
                    link(d.tensor_tensor(tmp, tmp, iota, ALU.add)),
                    link(d.tensor_reduce(idx, tmp, X_AXIS, ALU.min)),
                    link(d.tensor_tensor(out, tmp, b8(idx, out.shape[2]), ALU.is_equal)))
                link(d.tensor_reduce(g_max, lg[:, :, 0:4], X_AXIS, ALU.max))
                d.tensor_tensor(gd, lg[:, :, 0:4], b8(g_max, 4), ALU.subtract).then_inc(m_gx, 1)
                d.wait_ge(m_ex, 2 * l + 1)
                link(d.tensor_reduce(g_sum, ge, X_AXIS, ALU.add))
                link(d.reciprocal(g_w, g_sum))
                link(d.tensor_tensor(gm, lg[:, :, 0:4], b8(g_max, 4), ALU.is_equal))
                first(gm, ge, gm, iota4, i_)
                es, hit, oh1, oh2, tmp = r64
                gm4 = gm.unsqueeze(3).broadcast_to([P, 8, 4, 8])
                four = lambda x: x.rearrange("p t (g e) -> p t g e", g=4)
                link(d.tensor_tensor(four(r256[0]), four(lg[:, :, 4:36]), gm4, ALU.mult))
                link(d.tensor_reduce(es, r256[0].rearrange("p t (g e) -> p t e g", g=4), X_AXIS, ALU.add))
                link(d.tensor_reduce(v1, es, X_AXIS, ALU.max))
                link(d.tensor_tensor(hit, es, b8(v1, 8), ALU.is_equal))
                first(oh1, tmp, hit, iota8, i_)
                link(d.scalar_tensor_tensor(out=es, in0=oh1, scalar=NEG, in1=es, op0=ALU.mult, op1=ALU.add))
                link(d.tensor_reduce(v2, es, X_AXIS, ALU.max))
                link(d.tensor_tensor(hit, es, b8(v2, 8), ALU.is_equal))
                first(oh2, tmp, hit, iota8, i_)
                d.tensor_tensor(dv, v2, v1, ALU.subtract).then_inc(m_gx, 1)
                for oh, out in ((oh1, r256[0]), (oh2, r256[1])):
                    link(d.tensor_tensor(four(out), oh.unsqueeze(2).broadcast_to([P, 8, 4, 8]), gm4, ALU.mult))
                d.tensor_tensor(r256[2], r256[0], r256[1], ALU.add).then_inc(m_mk, 1)
                d.wait_ge(m_ex, 2 * l + 2)
                link(d.tensor_scalar(den, ev, 1.0, None, ALU.add))
                link(d.reciprocal(p1, den))
                link(d.tensor_tensor(moe_w[:, 0], p1, g_w, ALU.mult))
                link(d.tensor_tensor(moe_w[:, 1], moe_w[:, 0], ev, ALU.mult))
                d.wait_ge(m_rk, l + 1)
                link(d.tensor_copy(r256[3], bank(1)[:, 0:256].rearrange("p (t e) -> p t e", e=32)))
                counts = ends[0:32, 0:1]
                link(d.tensor_copy(counts, bank(6)[0:32, 0:1]))
                link(d.tensor_scalar(cmp_n[:, 0], c("full_blocks", 32), counts, None, ALU.is_lt))
                link(d.tensor_reduce(ends[0:32, 1:2], cmp_n[:, 0], X_AXIS, ALU.add))
                d.tensor_copy(n_blk, ends[0:32, 1:2].broadcast_to([32, 128])).then_inc(m_nb, 1)
                d.wait_ge(m_nb, l + 1)
                d.wait_ge(m_pb, l + 1)
                link(d.tensor_copy(ends, bank(7)[:, 0:64]))
                before = ends[:, 0:32].unsqueeze(1).broadcast_to([P, 8, 32])
                link(d.scalar_tensor_tensor(out=r256[3], in0=before, scalar=float(BLK), in1=r256[3],
                                            op0=ALU.mult, op1=ALU.add))
                for a in range(2):
                    link(d.tensor_tensor(r256[4], r256[a], r256[3], ALU.mult))
                    link(d.tensor_reduce(r8[a], r256[4], X_AXIS, ALU.add))
                    link(d.tensor_copy(moe_i[:, a], r8[a]))
                upto = ends[0:1, 32:64].unsqueeze(1).broadcast_to([1, NBLK, 32])
                n_b = c("iota_blk", 1).unsqueeze(2).broadcast_to([1, NBLK, 32])
                link(d.tensor_tensor(cmp_b, upto, n_b, ALU.is_le))
                link(d.tensor_reduce(tab_f[:, 0:NBLK], cmp_b, X_AXIS, ALU.add))
                link(d.tensor_scalar(tab_f[:, 0:NBLK], tab_f[:, 0:NBLK], float(E - 1), None, ALU.min))
                pairs = cmp_b.rearrange("p a b -> p (a b)")[:, 0:NBLK // 2]
                link(d.tensor_scalar(pairs, c("iota_pair", 1), ends[0:1, 63:64], None, ALU.is_lt))
                link(d.tensor_reduce(tab_f[:, NBLK:NBLK + 1], pairs, X_AXIS, ALU.add))
                d.tensor_copy(moe_tab[0:1, 0:NBLK + 1], tab_f[:, 0:NBLK + 1]).then_inc(m_tab, 1)
                d.wait_ge(m_ri, 16 * l + 16)
                d.tensor_copy(row_f, row_i).then_inc(m_rf, 1)
                d.wait_ge(m_rt, l + 1)
                d.tensor_copy(row_ix[0:BLK], bank(6)[0:BLK, 128:128 + NBLK])

            def pairs(self, eng):
                return eng.value_load(moe_tab[0:1, NBLK:NBLK + 1], min_val=1, max_val=NBLK // 2)

            def blocks_sp(self, sp):
                l = self.l
                n = self.pairs(sp)
                with sp.Fori(0, n) as j:
                    for s_ in range(2):
                        e = sp.value_load(moe_tab[0:1, bass.ds(2 * j + s_, 1)], min_val=0, max_val=E - 1)
                        wi = self.w_in[s_]
                        sp.wait_ge(self.gg, 2 * j + s_ + 1)
                        sp.dma_start(w_part[s_][0], t["w_gate"][l, bass.ds(e, 1)].rearrange(
                            "e (k p) n -> p (e k) n", p=P)).then_inc(wi[0], 16)
                        sp.wait_ge(self.gu, 2 * j + s_ + 1)
                        sp.dma_start(w_part[s_][1], t["w_up"][l, bass.ds(e, 1)].rearrange(
                            "e (k p) n -> p (e k) n", p=P)).then_inc(wi[1], 16)
                    for s_ in range(2):
                        e = sp.value_load(moe_tab[0:1, bass.ds(2 * j + s_, 1)], min_val=0, max_val=E - 1)
                        sp.wait_ge(self.yd, 4 * j + 2 * s_ + 2)
                        sp.dma_start(w_part[s_][2], t["w_down"][l, bass.ds(e, 1)].rearrange(
                            "e (k p) n -> p (e k) n", p=P)).then_inc(self.w_in[s_][2], 16)

            def blocks_pool(self, g):
                n = self.pairs(g)
                with g.Fori(0, n) as j:
                    for s_ in range(2):
                        g.wait_ge(self.xt, 2 * j + s_ + 1)
                        g.tensor_copy(moe_ix[0:BLK, s_:s_ + 1],
                                      row_ix[0:BLK, bass.ds(2 * j + s_, 1)]).then_inc(self.ix, 1)
                        g.wait_ge(self.ix, 2 * j + s_ + 1)
                        g.sem_inc(self.passed, 1)
                        g.indirect_dma_start(xb[0:BLK, s_], None, t["h_tok"],
                                             bass.IndirectOffsetOnAxis(ap=moe_ix[0:BLK, s_:s_ + 1], axis=0)
                                             ).then_inc(self.xg[s_], 16)

            def turned(self, s_, i, n=1):
                return bank(4 * s_ + i, n)

            def blocks_pe(self, pe):
                pe.sem_inc(self.xt, 2)
                pe.sem_inc(self.gg, 2)
                pe.sem_inc(self.gu, 2)
                pe.sem_inc(self.yd, 4)
                n = self.pairs(pe)
                with pe.Fori(0, n) as j:
                    for s_ in range(2):
                        pe.wait_ge(self.xg[s_], 16 * j + 16)
                        if s_ == 0:
                            pe.wait_ge(self.xe, 2 * j + 1)
                        else:
                            pe.wait_ge(self.hid, 2 * j + 2)
                        for k in range(KT):
                            last = pe.transpose(self.turned(s_, k // 4)[:, k % 4 * BLK:(k % 4 + 1) * BLK],
                                                xb[0:BLK, s_, 128 * k:128 * k + 128], ident[0:BLK, 0:BLK])
                        last.then_inc(self.xt, 1)
                    for s_ in range(2):
                        pe.wait_ge(self.xe, 2 * j + s_ + 2)
                        for part in range(2):
                            pe.wait_ge(self.w_in[s_][part], 16 * j + 16)
                            if part == 1 and s_ == 0:
                                pe.wait_ge(self.xe, 2 * j + 3)
                            for m in range(4):
                                for k in range(KT):
                                    last = pe.matmul(bank(2 + s_ + 2 * part)[:, BLK * m:BLK * m + BLK],
                                                     w_part[s_][part][:, k, 128 * m:128 * m + 128], xbT[:, s_, k],
                                                     start=k == 0, stop=k == KT - 1)
                            if part == 0:
                                last.then_inc(self.gg, 1)
                            else:
                                last.then_inc(self.gu, 1)
                    for s_ in range(2):
                        pe.wait_ge(self.hid, 2 * j + s_ + 3)
                        pe.wait_ge(self.w_in[s_][2], 16 * j + 16)
                        for half in range(2):
                            pe.wait_ge(self.ye[half], 2 * j + s_ + 1)
                            for k in range(4):
                                last = pe.matmul(bank(6 + half)[0:BLK, :], hid[:, s_, k],
                                                 w_part[s_][2][:, k, 512 * half:512 * half + 512],
                                                 start=k == 0, stop=k == 3)
                            last.then_inc(self.yd, 1)

            def blocks_act(self, a):
                a.sem_inc(self.ye[0], 1)
                for s_ in range(2):
                    a.sem_inc(self.yw[s_], 16)
                n = self.pairs(a)
                with a.Fori(0, n) as j:
                    for s_ in range(2):
                        a.wait_ge(self.gg, 2 * j + s_ + 3)
                        a.activation(sg[:, s_], bank(2 + s_)[:, 0:4 * BLK], ACT.Silu).then_inc(self.sg, 1)
                    for s_ in range(2):
                        a.wait_ge(self.yd, 4 * j + 2 * s_ + 5)
                        a.wait_ge(self.yw[s_], 16 * j + 16)
                        a.activation(y_sb[0:BLK, s_, 0:512], bank(6)[0:BLK], ACT.Copy).then_inc(self.ye[0], 1)
                        a.wait_ge(self.ye[0], 2 * j + s_ + 2)
                        a.wait_ge(self.ye[1], 2 * j + s_ + 2)
                        a.dma_start(t["y_tok"][bass.ds((2 * j + s_) * BLK, BLK), :],
                                    y_sb[0:BLK, s_]).then_inc(self.yw[s_], 16)
                for s_ in range(2):
                    a.wait_ge(self.yw[s_], 16 * n + 16)
                    a.sem_inc(self.passed, 1)

            def blocks_dve(self, d):
                d.sem_inc(self.xe, 1)
                d.sem_inc(self.hid, 2)
                d.sem_inc(self.ye[1], 1)
                n = self.pairs(d)
                with d.Fori(0, n) as j:
                    for s_ in range(2):
                        d.wait_ge(self.xt, 2 * j + s_ + 3)
                        d.wait_ge(self.gu, 2 * j + s_ + 1)
                        d.tensor_copy(xbT[:, s_].rearrange("p (b k) n -> p b (k n)", b=2),
                                      self.turned(s_, 0, 2).rearrange("p (b n) -> p b n", b=2)[:, :, 0:4 * BLK]
                                      ).then_inc(self.xe, 1)
                    for s_ in range(2):
                        d.wait_ge(self.sg, 2 * j + s_ + 1)
                        d.wait_ge(self.gu, 2 * j + s_ + 3)
                        d.tensor_tensor(hid[:, s_].rearrange("p k n -> p (k n)"), sg[:, s_],
                                        bank(4 + s_)[:, 0:4 * BLK], ALU.mult).then_inc(self.hid, 1)
                    for s_ in range(2):
                        d.wait_ge(self.yd, 4 * j + 2 * s_ + 6)
                        d.wait_ge(self.yw[s_], 16 * j + 16)
                        d.tensor_copy(y_sb[0:BLK, s_, 512:1024], bank(7)[0:BLK]).then_inc(self.ye[1], 1)

            def sum_pool(self, g):
                for i in range(KT):
                    if i >= 2:
                        g.wait_ge(m_cc, KT * self.l + i - 1)
                    for a in range(2):
                        g.indirect_dma_start(y_g[:, 2 * (i % 2) + a], None, t["y_tok"],
                                             bass.IndirectOffsetOnAxis(ap=moe_i[:, a, i:i + 1], axis=0)
                                             ).then_inc(m_cg[i % 2], 16)

            def sum_dve(self, d, link):
                l = self.l
                for i in range(KT + 1):
                    if i < KT:
                        d.wait_ge(m_cg[i % 2], 32 * (KT // 2 * l + i // 2 + 1))
                        if i >= 2:
                            d.wait_ge(m_ct, KT * l + i - 1)
                        link(d.tensor_scalar(y_s[:, i % 2], y_g[:, 2 * (i % 2)], moe_w[:, 0, i:i + 1], None, ALU.mult))
                        d.scalar_tensor_tensor(out=y_s[:, i % 2], in0=y_g[:, 2 * (i % 2) + 1],
                                               scalar=moe_w[:, 1, i:i + 1], in1=y_s[:, i % 2], op0=ALU.mult,
                                               op1=ALU.add).then_inc(m_cc, 1)
                    if i:
                        d.wait_ge(m_ct, KT * l + i)
                        b = bank(2 * ((i - 1) % 2), 2)
                        for k in range(KT):
                            x = x_l[:, k, 128 * (i - 1):128 * i]
                            last = d.scalar_tensor_tensor(out=x, in0=b[:, 128 * k:128 * k + 128],
                                                          scalar=mod[f"l{l}"][:, 40 + k, 0:1], in1=x,
                                                          op0=ALU.mult, op1=ALU.add)
                        last.then_inc(m_cx, 1)

            def sum_pe(self, pe):
                for i in range(KT):
                    pe.wait_ge(m_cc, KT * self.l + i + 1)
                    if i >= 2:
                        pe.wait_ge(m_cx, KT * self.l + i - 1)
                    b = bank(2 * (i % 2), 2)
                    for k in range(KT):
                        last = pe.transpose(b[:, 128 * k:128 * k + 128], y_s[:, i % 2, 128 * k:128 * k + 128], ident)
                    last.then_inc(m_ct, 1)

        M = [Moe(0), Moe(1)]
        out_done = sem("out_done")
        zeros = mem(STAGE + 10240, D)
        z_set, z_ld = sem("z_set"), sem("z_ld")
        v_chain, at_ld, c2_ld = sem("v_chain"), sem("at_ld"), sem("c2_ld")

        @block.sync
        def _(sp):
            sp.dma_start(vec, t["vec"]).then_inc(loaded, 16)
            sp.dma_start(cst, t["const"]).then_inc(loaded, 16)
            sp.dma_start(x_l, t["x"].rearrange("(k p) n -> p k n", p=P)).then_inc(loaded, 16)
            sp.dma_start(x_c, t["ctx"].rearrange("(k p) n -> p k n", p=P)).then_inc(loaded, 16)
            for n, (name, j, mat, col, width) in enumerate(units):
                if n == UNITS_TO_MOE0 + 2:
                    sp.wait_ge(stage_end, closed("m0_route"))
                    M[0].blocks_sp(sp)
                if n >= 2:
                    sp.wait_ge(*unit_used[n - 2])
                dst = ring[:, n % 2].rearrange("p (k n) -> p k n", k=KT)[:, :, 0:width]
                sp.dma_start(dst, mat[:, col:col + width].rearrange("(k p) n -> p k n", p=P)
                             ).then_inc(ring_in[n % 2], 16)
            sp.wait_ge(stage_end, closed("m1_route"))
            M[1].blocks_sp(sp)
            sp.wait_ge(stage_end, closed("final2"))
            sp.dma_start(t["out"].rearrange("(k p) n -> p k n", p=P), x_l).then_inc(out_done, 16)
            sp.wait_ge(out_done, 16)

        @block.tensor
        def _(pe):
            close = closer(pe)
            pe.wait_ge(loaded, 64)
            close("loads")
            for _ in mod_pe(pe, 0):
                pass
            close("ab_mod")
            N_AB.pe(pe)
            close("ab_norm")
            P_AB_A.pe(pe)
            close("ab_gated")
            P_AB_Q.pe(pe)
            close("ab_qkv")
            hd_pe(pe)
            close("ab_heads")
            A_AB.pe(pe, mod_col_pe(pe))
            close("ab_attn")
            ln_pe(pe)
            close("ab_ln")
            P_AB_Z.pe(pe)
            close("ab_z")
            P_AB_O.pe(pe)
            close("ab_out")
            N_CD.pe(pe)
            close("cd_norm")
            P_CD_F.pe(pe)
            close("cd_f")
            four_pe(pe)
            close("cd_four")
            P_CD_Q.pe(pe)
            close("cd_qkv")
            A_CD.pe(pe)
            close("cd_attn")
            P_CD_Z.pe(pe)
            close("cd_z")
            P_CD_O.pe(pe)
            close("cd_out")
            N_F1.pe(pe)
            close("final1")
            N_L0.pe(pe)
            close("ev_norm")
            P_EV.pe(pe)
            close("ev_in")
            rope_pe(pe)
            close("ev_rope")
            A_EV.pe(pe)
            close("ev_attn")
            sgu_pe(pe)
            close("ev_sgu")
            P_EV_O.pe(pe)
            close("ev_out")
            N_L0B.pe(pe)
            close("m0_norm")
            M[0].route_pe(pe)
            close("m0_route")
            M[0].blocks_pe(pe)
            close("m0_blocks")
            M[0].sum_pe(pe)
            close("m0_sum")
            N_L1.pe(pe)
            close("od_norm")
            P_OD.pe(pe)
            close("od_in")
            close("od_conv")
            P_OD_O.pe(pe)
            close("od_out")
            N_L1B.pe(pe)
            close("m1_norm")
            M[1].route_pe(pe)
            close("m1_route")
            M[1].blocks_pe(pe)
            close("m1_blocks")
            M[1].sum_pe(pe)
            close("m1_sum")
            N_F2.pe(pe)
            close("final2")

        @block.scalar
        def _(a):
            close = closer(a)
            a.wait_ge(loaded, 64)
            a.activation(silu_c, v("silu_in", 0, 32), ACT.Silu)
            close("loads")
            close("ab_mod")
            N_AB.act(a)
            close("ab_norm")
            P_AB_A.act(a)
            close("ab_gated")
            P_AB_Q.act(a)
            close("ab_qkv")
            hd_act(a)
            close("ab_heads")
            A_AB.act(a)
            close("ab_attn")
            ln_act(a)
            close("ab_ln")
            P_AB_Z.act(a)
            close("ab_z")
            close("ab_out")
            N_CD.act(a)
            close("cd_norm")
            P_CD_F.act(a)
            close("cd_f")
            four_act(a)
            close("cd_four")
            P_CD_Q.act(a)
            close("cd_qkv")
            A_CD.act(a)
            close("cd_attn")
            P_CD_Z.act(a)
            close("cd_z")
            close("cd_out")
            N_F1.act(a)
            close("final1")
            N_L0.act(a)
            close("ev_norm")
            P_EV.act(a)
            close("ev_in")
            close("ev_rope")
            a.wait_ge(at_ld, 32)
            A_EV.act(a)
            close("ev_attn")
            sgu_act(a)
            close("ev_sgu")
            close("ev_out")
            N_L0B.act(a)
            close("m0_norm")
            M[0].route_act(a)
            close("m0_route")
            M[0].blocks_act(a)
            close("m0_blocks")
            close("m0_sum")
            N_L1.act(a)
            close("od_norm")
            P_OD.act(a)
            close("od_in")
            close("od_conv")
            close("od_out")
            N_L1B.act(a)
            close("m1_norm")
            M[1].route_act(a)
            close("m1_route")
            M[1].blocks_act(a)
            close("m1_blocks")
            close("m1_sum")
            N_F2.act(a)
            close("final2")

        @block.vector
        def _(d):
            chain = [0]

            def link(ins):
                chain[0] += 1
                ins.then_inc(v_chain, 1)
                d.wait_ge(v_chain, chain[0])

            close = closer(d)
            d.wait_ge(loaded, 64)
            close("loads")
            mod_dve(d, link, 0)
            close("ab_mod")
            N_AB.dve(d)
            close("ab_norm")
            P_AB_A.dve(d)
            close("ab_gated")
            P_AB_Q.dve(d)
            close("ab_qkv")
            hd_dve(d, link)
            close("ab_heads")
            A_AB.dve(d, link, conv_and_mods(d))
            close("ab_attn")
            for i in (1, 2, 3):
                mod_dve(d, link, i)
            ln_dve(d)
            close("ab_ln")
            P_AB_Z.dve(d)
            close("ab_z")
            P_AB_O.dve(d)
            close("ab_out")
            N_CD.dve(d)
            close("cd_norm")
            P_CD_F.dve(d)
            close("cd_f")
            four_dve(d, link)
            close("cd_four")
            P_CD_Q.dve(d)
            close("cd_qkv")
            A_CD.dve(d, link)
            close("cd_attn")
            P_CD_Z.dve(d)
            close("cd_z")
            P_CD_O.dve(d)
            close("cd_out")
            N_F1.dve(d)
            close("final1")
            N_L0.dve(d)
            close("ev_norm")
            P_EV.dve(d)
            close("ev_in")
            rope_dve(d, link)
            close("ev_rope")
            d.wait_ge(at_ld, 32)
            A_EV.dve(d, link)
            close("ev_attn")
            sgu_dve(d, link)
            close("ev_sgu")
            P_EV_O.dve(d)
            close("ev_out")
            N_L0B.dve(d)
            close("m0_norm")
            M[0].route_dve(d, link)
            close("m0_route")
            M[0].blocks_dve(d)
            close("m0_blocks")
            M[0].sum_dve(d, link)
            close("m0_sum")
            N_L1.dve(d)
            close("od_norm")
            P_OD.dve(d)
            close("od_in")
            conv3_dve(d, link)
            close("od_conv")
            P_OD_O.dve(d)
            close("od_out")
            N_L1B.dve(d)
            close("m1_norm")
            M[1].route_dve(d, link)
            close("m1_route")
            M[1].blocks_dve(d)
            close("m1_blocks")
            M[1].sum_dve(d, link)
            close("m1_sum")
            N_F2.dve(d)
            close("final2")

        @block.gpsimd
        def _(g):
            close = closer(g)
            g.wait_ge(loaded, 64)
            close("loads")
            close("ab_mod")
            for ct in range(4):
                for a0, n in ((0, HALF), (HALF + S, 2 * HALF), (S + L + 3 * HALF, HALF)):
                    g.memset(G_U[:, ct, a0:a0 + n], 0.0)
            close("ab_norm")
            g.memset(zeros, 0.0).then_inc(z_set, 1)
            g.wait_ge(z_set, 1)
            g.dma_start(t["y_tok"].rearrange("(b r) n -> r b n", r=BLK),
                        zeros[0:BLK].unsqueeze(1).broadcast_to([BLK, NBLK, D])).then_inc(z_ld, 16)
            g.wait_ge(z_ld, 16)
            close("ab_gated")
            g.dma_start(rope, t["rope_ab"].rearrange("p (a b) -> p a b", a=2)).then_inc(hd_ld, 16)
            close("ab_qkv")
            g.memset(mod_to, 0.0).then_inc(mod_to_set, 1)
            g.wait_ge(mod_to_set, 1)
            g.memset(mod_to[:, 1:2], 1.0)
            close("ab_heads")
            close("ab_attn")
            close("ab_ln")
            g.dma_start(x_c, t["ctx"].rearrange("(k p) n -> p k n", p=P)).then_inc(c2_ld, 16)
            g.wait_ge(c2_ld, 16)
            close("ab_z")
            close("ab_out")
            close("cd_norm")
            close("cd_f")
            four_pool(g)
            close("cd_four")
            close("cd_qkv")
            close("cd_attn")
            g.dma_start(x_c, t["ctx2"].rearrange("(k p) n -> p k n", p=P)).then_inc(c2_ld, 16)
            g.wait_ge(c2_ld, 32)
            close("cd_z")
            close("cd_out")
            close("final1")
            close("ev_norm")
            g.dma_start(rope_e, t["rope_ev"].rearrange("p (a b) -> p a b", a=2)).then_inc(ev_ld, 16)
            close("ev_in")
            close("ev_rope")
            g.dma_start(wmask, t["win_mask"]).then_inc(at_ld, 16)
            g.dma_start(sinkc, t["sink"].partition_broadcast(P)).then_inc(at_ld, 16)
            close("ev_attn")
            sgu_pool(g)
            close("ev_sgu")
            close("ev_out")
            close("m0_norm")
            M[0].route_pool(g)
            close("m0_route")
            M[0].blocks_pool(g)
            close("m0_blocks")
            M[0].sum_pool(g)
            close("m0_sum")
            for ct in range(KT):
                for a0 in (0, S + 1):
                    g.memset(prod[:, ct, a0:a0 + 1], 0.0)
            close("od_norm")
            close("od_in")
            close("od_conv")
            close("od_out")
            close("m1_norm")
            M[1].route_pool(g)
            close("m1_route")
            M[1].blocks_pool(g)
            close("m1_blocks")
            M[1].sum_pool(g)
            close("m1_sum")
            close("final2")


STAGES = ["loads", "ab_mod", "ab_norm", "ab_gated", "ab_qkv", "ab_heads", "ab_attn", "ab_ln", "ab_z",
          "ab_out", "cd_norm", "cd_f", "cd_four", "cd_qkv", "cd_attn", "cd_z", "cd_out", "final1", "ev_norm",
          "ev_in", "ev_rope", "ev_attn", "ev_sgu", "ev_out", "m0_norm", "m0_route", "m0_blocks", "m0_sum",
          "od_norm", "od_in", "od_conv", "od_out", "m1_norm", "m1_route", "m1_blocks", "m1_sum", "final2"]


def closed(name):
    return 4 * (STAGES.index(name) + 1)


def columns(x):
    return x.reshape(-1, P).T


def constants():
    i = np.arange(P)
    c = {"ident": np.eye(P), "ones": np.ones((P, P)), "before": i[:, None] < i[None, :]}
    swap = np.zeros((P, P))
    even = i[i % 2 == 0]
    swap[even + 1, even] = -1
    swap[even, even + 1] = 1
    c["swap_ab"] = swap
    swap = np.zeros((P, P))
    low = i[i % 32 < 16]
    swap[low + 16, low] = -1
    swap[low, low + 16] = 1
    c["swap_ev"] = swap
    c["head_ones"] = i[:, None] // HEAD == i[None, :] // HEAD
    e = np.arange(E)
    z = np.zeros((P, E))
    z[:E] = e[:, None] < e[None, :]
    c["expert_before"] = z.copy()
    z[:E] = e[:, None] <= e[None, :]
    c["expert_upto"] = z
    row = lambda x: np.broadcast_to(x, (P, len(x)))
    c["full_blocks"] = row(BLK * np.arange(S // BLK + 1))
    c["iota4"], c["iota8"] = row(64 + np.arange(4)), row(64 + np.arange(8))
    c["iota_blk"], c["iota_pair"] = row(np.arange(NBLK)), row(2 * np.arange(NBLK // 2))
    c["eps"] = np.full((P, 1), EPS)
    const = np.concatenate([np.asarray(c[n], np.float32) for n in CONST], axis=1)

    tok = np.arange(S)
    inv = 10000.0 ** (-np.arange(16, dtype=np.float64) / 16)
    ang = np.concatenate([(tok // GRID)[:, None] * inv, (tok % GRID)[:, None] * inv], axis=1)
    a = ang[:, (i % HEAD) // 2].T
    d = i % HEAD
    b = ang[:, 16 * (d // 32) + d % 16].T
    f32 = np.float32
    rope_ab = np.concatenate([np.cos(a), np.sin(a)], axis=1).astype(f32)
    rope_ev = np.concatenate([np.cos(b), np.sin(b)], axis=1).astype(f32)

    th = 2 * np.pi * ((tok[:, None] * tok[None, :]) % S) / S
    tc = 2 * np.pi * ((i[:, None] * i[None, :]) % P) / P
    norm = 1 / np.sqrt(S * P)
    w = np.arange(GRID)
    cs = np.clip(w - NA_COLS // 2, 0, GRID - NA_COLS)
    ok = (w[None, :] >= cs[:, None]) & (w[None, :] < cs[:, None] + NA_COLS)
    na = np.where(ok, 0.0, NEG)
    q = np.arange(P)
    win = np.zeros((P, 768))
    win[:, 0:128] = np.where(q[None, :] >= q[:, None], 0, NEG)
    win[:, 512 + 0:512 + 128] = np.where(q[None, :] <= q[:, None], 0, NEG)
    e_sp = np.zeros((8, 4, P))
    for h in range(8):
        e_sp[h, h // 2, 64 * (h % 2):64 * (h % 2) + 64] = 1
    return dict(const=const, rope_ab=rope_ab, rope_ev=rope_ev, four_cos=np.cos(th).astype(f32),
                four_sin=np.sin(th).astype(f32),
                four_ch=np.concatenate([np.cos(tc) * norm, np.sin(tc) * norm], axis=1).astype(f32),
                na_mask=np.concatenate([na, na]).astype(f32), win_mask=win.astype(f32),
                e_sp=e_sp.reshape(8, 512).astype(f32),
                tok_id=(i[:, None] + P * np.arange(KT)[None, :]).astype(np.int32))


def kernel(**inp):
    import concourse.bacc as bacc
    from concourse.bass_utils import run_bass_kernel_spmd as run

    x = {k: np.asarray(a) for k, a in inp.items()}
    heads = np.arange(512).reshape(8, 64)
    pairs = np.concatenate([np.concatenate([heads[i], heads[i + 4]]) for i in range(4)])
    t128 = np.arange(128)
    gated = np.concatenate([np.concatenate([512 + 128 * i + t128, 128 * i + t128]) for i in range(4)])
    y_ab = np.concatenate([np.arange(512), 512 + pairs])
    y_ev = np.concatenate([pairs, np.arange(512, 1024)])
    ab_cols = np.concatenate([gated, 1024 + pairs, np.arange(1536, 1792), 1792 + y_ab])
    ev_cols = np.concatenate([pairs, np.arange(512, 1792)])
    od_cols = np.concatenate([np.concatenate([1024 + 128 * i + t128, 2048 + 128 * i + t128, 128 * i + t128])
                              for i in range(8)])
    vecs = {
        "ab_b_ada": columns(x["ab_b_ada"][0]), "ab_norm_g": columns(x["ab_norm_g"][0]),
        "ab_conv_w": x["ab_conv_w"][0].reshape(TAPS, 4, P).transpose(2, 1, 0).reshape(P, 4 * TAPS),
        "ab_conv_b": columns(x["ab_conv_b"][0]), "ab_ln_g": columns(x["ab_ln_g"][0]),
        "ab_ln_b": columns(x["ab_ln_b"][0]), "ab_qn_g": np.tile(x["ab_q_norm_g"][0], 2)[:, None],
        "ab_kn_g": np.tile(x["ab_k_norm_g"][0], 2)[:, None], "cd_b_ada": columns(x["cd_b_ada"][0]),
        "cd_norm_g": columns(x["cd_norm_g"][0]), "final_g": columns(x["final_norm_g"]),
        "b_ada0": columns(x["b_ada_2"][0]), "b_ada1": columns(x["b_ada_2"][1]),
        "g_norm1_0": columns(x["g_norm1_2"][0]), "g_norm1_1": columns(x["g_norm1_2"][1]),
        "g_norm2_0": columns(x["g_norm2_2"][0]), "g_norm2_1": columns(x["g_norm2_2"][1]),
        "g_final2": columns(x["g_final_2"]),
        "conv3_w": x["conv_w_2"][0].reshape(3, KT, P).transpose(2, 1, 0).reshape(P, 24),
        "silu_in": np.stack([np.stack([x["c"][0], x["c_ctx"]]), np.stack([x["c_2"][0], x["c_ctx_2"]])])
        .reshape(2, 2, KT, P).transpose(3, 0, 2, 1).reshape(P, 32),
    }
    arrays = constants()
    arrays.update(
        vec=np.concatenate([vecs[n] for n in VEC], axis=1),
        x=x["x"][0].T, ctx=x["ctx"][0].T, ctx2=x["ctx_2"][0].T,
        ab_w_ada=x["ab_w_ada"][0], ab_w_in=x["ab_w_in"][0][:, ab_cols], ab_w_out=x["ab_w_out"][0][y_ab],
        cd_w_ada=x["cd_w_ada"][0], cd_w_in=x["cd_w_in"][0], cd_w_out=x["cd_w_out"][0],
        w_four=x["cd_w_fourier"][0],
        rpb_pad=np.pad(x["cd_rpb"][0][:, :, ::-1], ((0, 0), (0, 0), (48, 48))),
        w_ada0=x["w_ada_2"][0], w_ada1=x["w_ada_2"][1],
        w_in_even=x["w_in_even_2"][0][:, ev_cols], w_out_even=x["w_out_even_2"][0][y_ev],
        sink=x["attn_sink_2"][0], g_sgu=x["g_sgu_2"][0],
        w_sp=x["w_spatial_2"][0].transpose(2, 0, 1).reshape(P, 8 * P), b_sp=x["b_spatial_2"][0],
        w_in_odd=x["w_in_odd_2"][0][:, od_cols], w_out_odd=x["w_out_odd_2"][0],
        w_router=np.concatenate([x["w_router_group_2"], x["w_router_expert_2"]], axis=2),
        b_router=np.concatenate([x["b_router_group_2"], x["b_router_expert_2"]], axis=1),
        w_gate=x["w_gate_2"], w_up=x["w_up_2"], w_down=x["w_down_2"],
    )
    nc = bacc.Bacc("TRN2", target_bir_lowering=False, num_devices=1)
    arrays = {k: np.ascontiguousarray(a) for k, a in arrays.items()}
    t = {k: nc.dram_tensor(f"in_{k}", a.shape, mybir.dt.from_np(a.dtype), kind="ExternalInput").ap()
         for k, a in arrays.items()}
    t["row_tok"] = nc.dram_tensor("row_tok", (NBLK * BLK, 1), I32, kind="Internal").ap()
    t["h_tok"] = nc.dram_tensor("h_tok", (S, D), F32, kind="Internal").ap()
    t["y_tok"] = nc.dram_tensor("y_tok", (NBLK * BLK, D), F32, kind="Internal").ap()
    t["out"] = nc.dram_tensor("out_x", (D, S), F32, kind="ExternalOutput").ap()
    program(nc, t)
    r = run(nc, [{f"in_{k}": a for k, a in arrays.items()}], core_ids=[0])
    return np.ascontiguousarray(r.results[0]["out_x"].T)[None]
```
